# Optimizing a Trainium2 kernel written in Bass

```python
import jax, jax.numpy as jnp
from jax import lax
import numpy as np

D_MODEL = 1024
BATCH = 1
SEQ = 256
DEPTH = 2

N_EVEN = (DEPTH + 1) // 2
N_ODD = DEPTH // 2

SB_HEADS = 8
SB_HEAD_DIM = 64
SB_WIDTH = SB_HEADS * SB_HEAD_DIM
Q_BLOCK = 128
CONV_WIDTH = D_MODEL // 2
CONV_KERNEL = 31
EVEN_IN = 3 * SB_WIDTH + 2 * CONV_WIDTH
EVEN_MIX = SB_WIDTH + CONV_WIDTH
POOL_WINDOWS = (2, 4, 8, 16)
POOL_GROUP = D_MODEL // len(POOL_WINDOWS)
N_EXPERTS = 64
TOP_K = 8
N_GROUPS = 8
TOPK_GROUPS = 4
EXPERT_FF = 256
SHARED_FF = 256
ROUTED_SCALE = 2.5
MOE_BLOCK = 256
EPS = 1e-6

kernel_name = "hybrid_sb_conformer_pool_moe_adaln"

def rmsnorm(x, g):
    xf = x.astype(jnp.float32)
    y = xf * lax.rsqrt(jnp.mean(xf * xf, axis=-1, keepdims=True) + EPS)
    return (y * g.astype(jnp.float32)).astype(x.dtype)

def layernorm(x, g, b):
    xf = x.astype(jnp.float32)
    mu = jnp.mean(xf, axis=-1, keepdims=True)
    var = jnp.mean(jnp.square(xf - mu), axis=-1, keepdims=True)
    y = (xf - mu) * lax.rsqrt(var + EPS)
    return (y * g.astype(jnp.float32) + b.astype(jnp.float32)).astype(x.dtype)

def modulate(h, shift, scale):
    return h * (1 + scale) + shift

def stick_breaking_attention(q, k, v):
    S = q.shape[1]
    scale = SB_HEAD_DIM ** -0.5
    outs = []
    for i in range(S // Q_BLOCK):
        t0, t1 = i * Q_BLOCK, (i + 1) * Q_BLOCK
        qb, kb, vb = q[:, t0:t1], k[:, :t1], v[:, :t1]
        z = jnp.einsum('bqhd,bkhd->bhqk', qb, kb).astype(jnp.float32) * scale
        causal = jnp.arange(t1)[None, :] < jnp.arange(t0, t1)[:, None]
        log_beta = jax.nn.log_sigmoid(z)
        log_1m = jnp.where(causal, jax.nn.log_sigmoid(-z), 0.0)
        log_rem = lax.cumsum(log_1m, axis=3, reverse=True) - log_1m
        a = jnp.where(causal, jnp.exp(log_beta + log_rem), 0.0)
        outs.append(jnp.einsum('bhqk,bkhd->bqhd', a.astype(vb.dtype), vb))
    return jnp.concatenate(outs, axis=1)

def causal_depthwise_conv(u, w, b):
    y = lax.conv_general_dilated(u, w, window_strides=(1,), padding=[(CONV_KERNEL - 1, 0)],
                                 dimension_numbers=('NWC', 'WIO', 'NWC'),
                                 feature_group_count=u.shape[-1])
    return y + b

def even_mixer(h, w_in, dw_w, dw_b, ln_g, ln_b, w_out):
    B, S, _ = h.shape
    proj = h @ w_in
    q = proj[..., 0:SB_WIDTH].reshape(B, S, SB_HEADS, SB_HEAD_DIM)
    k = proj[..., SB_WIDTH:2 * SB_WIDTH].reshape(B, S, SB_HEADS, SB_HEAD_DIM)
    v = proj[..., 2 * SB_WIDTH:3 * SB_WIDTH].reshape(B, S, SB_HEADS, SB_HEAD_DIM)
    a_val = proj[..., 3 * SB_WIDTH:3 * SB_WIDTH + CONV_WIDTH]
    a_gate = proj[..., 3 * SB_WIDTH + CONV_WIDTH:]
    att = stick_breaking_attention(q, k, v).reshape(B, S, SB_WIDTH)
    u = a_val * jax.nn.sigmoid(a_gate)
    u = causal_depthwise_conv(u, dw_w, dw_b)
    u = jax.nn.silu(layernorm(u, ln_g, ln_b))
    return jnp.concatenate([att, u], axis=-1) @ w_out

def trailing_mean(u, w):
    S = u.shape[1]
    cs = jnp.cumsum(u.astype(jnp.float32), axis=1)
    prev = jnp.pad(cs, ((0, 0), (w, 0), (0, 0)))[:, :S]
    cnt = jnp.minimum(jnp.arange(1, S + 1), w).astype(jnp.float32)[None, :, None]
    return ((cs - prev) / cnt).astype(u.dtype)

def odd_mixer(h, w_in, w_grp, ch_scale, w_out):
    u = h @ w_in
    outs = []
    for gi, w in enumerate(POOL_WINDOWS):
        ug = u[..., gi * POOL_GROUP:(gi + 1) * POOL_GROUP]
        pooled = trailing_mean(ug, w) - ug
        outs.append(jnp.einsum('bsc,cd->bsd', pooled, w_grp[gi]))
    y = jnp.concatenate(outs, axis=-1) * ch_scale
    return y @ w_out

def route(xf, w_router, bias):
    N = xf.shape[0]
    per_group = N_EXPERTS // N_GROUPS
    scores = jax.nn.sigmoid(xf.astype(jnp.float32) @ w_router.astype(jnp.float32))
    biased = scores + bias.astype(jnp.float32)
    grp_score = lax.top_k(biased.reshape(N, N_GROUPS, per_group), 2)[0].sum(-1)
    _, gidx = lax.top_k(grp_score, TOPK_GROUPS)
    gmask = jax.nn.one_hot(gidx, N_GROUPS, dtype=jnp.float32).sum(axis=1) > 0
    emask = jnp.repeat(gmask, per_group, axis=1)
    _, idx = lax.top_k(jnp.where(emask, biased, -jnp.inf), TOP_K)
    wts = jnp.take_along_axis(scores, idx, axis=1)
    wts = wts / jnp.sum(wts, axis=-1, keepdims=True) * ROUTED_SCALE
    return idx, wts

def routed_experts(xf, idx, wts, w1, w3, w2):
    N, D = xf.shape
    M = N * TOP_K
    flat_e = idx.reshape(-1)
    flat_tok = jnp.arange(M, dtype=jnp.int32) // TOP_K
    flat_w = wts.reshape(-1)
    order = jnp.argsort(flat_e)
    e_s, tok_s, w_s = flat_e[order], flat_tok[order], flat_w[order]
    counts = jnp.bincount(flat_e, length=N_EXPERTS)
    padded = (counts + MOE_BLOCK - 1) // MOE_BLOCK * MOE_BLOCK
    pend = jnp.cumsum(padded)
    pstart = pend - padded
    gstart = jnp.cumsum(counts) - counts
    dest = pstart[e_s] + (jnp.arange(M) - gstart[e_s])
    n_blocks = (M + MOE_BLOCK - 1) // MOE_BLOCK + N_EXPERTS
    P = n_blocks * MOE_BLOCK
    slot_tok = jnp.full((P,), N, dtype=jnp.int32).at[dest].set(tok_s)
    slot_w = jnp.zeros((P,), jnp.float32).at[dest].set(w_s)
    block_e = jnp.clip(jnp.searchsorted(pend, jnp.arange(n_blocks) * MOE_BLOCK, side='right'),
                       0, N_EXPERTS - 1)
    xpad = jnp.concatenate([xf, jnp.zeros((1, D), xf.dtype)], axis=0)

    def body(acc, blk):
        tok_b, w_b, e = blk
        xb = xpad[tok_b]
        hb = jax.nn.silu(xb @ w1[e]) * (xb @ w3[e])
        yb = (hb @ w2[e]).astype(jnp.float32) * w_b[:, None]
        return acc.at[tok_b].add(yb), None

    acc, _ = lax.scan(body, jnp.zeros((N + 1, D), jnp.float32),
                      (slot_tok.reshape(n_blocks, MOE_BLOCK), slot_w.reshape(n_blocks, MOE_BLOCK), block_e))
    return acc[:N]

def moe_ffn(h, w_router, bias, w1, w3, w2, s1, s3, s2):
    B, S, D = h.shape
    xf = h.reshape(B * S, D)
    idx, wts = route(xf, w_router, bias)
    routed = routed_experts(xf, idx, wts, w1, w3, w2)
    shared = (jax.nn.silu(xf @ s1) * (xf @ s3)) @ s2
    return (shared.astype(jnp.float32) + routed).astype(h.dtype).reshape(B, S, D)

def setup_inputs(seed: int = 0) -> dict:
    key = jax.random.key(seed)
    ks = jax.random.split(key, 26)
    f32 = jnp.float32
    D = D_MODEL
    nrm = lambda k, shape, fan: jax.random.normal(k, shape, f32) * (fan ** -0.5)
    rnd = lambda k, shape, s: s * jax.random.normal(k, shape, f32)
    return {
        "x": jax.random.normal(ks[0], (BATCH, SEQ, D), f32),
        "c": jax.random.normal(ks[1], (BATCH, D), f32),
        "ada_w": rnd(ks[2], (DEPTH, D, 6 * D), 0.01),
        "ada_b": rnd(ks[3], (DEPTH, 6 * D), 0.02),
        "norm1_g": 1.0 + rnd(ks[4], (DEPTH, D), 0.05),
        "norm2_g": 1.0 + rnd(ks[5], (DEPTH, D), 0.05),
        "ev_w_in": nrm(ks[6], (N_EVEN, D, EVEN_IN), D),
        "ev_dw_w": nrm(ks[7], (N_EVEN, CONV_KERNEL, 1, CONV_WIDTH), CONV_KERNEL),
        "ev_dw_b": rnd(ks[8], (N_EVEN, CONV_WIDTH), 0.02),
        "ev_ln_g": 1.0 + rnd(ks[9], (N_EVEN, CONV_WIDTH), 0.05),
        "ev_ln_b": rnd(ks[10], (N_EVEN, CONV_WIDTH), 0.02),
        "ev_w_out": nrm(ks[11], (N_EVEN, EVEN_MIX, D), EVEN_MIX),
        "od_w_in": nrm(ks[12], (N_ODD, D, D), D),
        "od_w_grp": nrm(ks[13], (N_ODD, len(POOL_WINDOWS), POOL_GROUP, POOL_GROUP), POOL_GROUP),
        "od_scale": 1.0 + rnd(ks[14], (N_ODD, D), 0.1),
        "od_w_out": nrm(ks[15], (N_ODD, D, D), D),
        "moe_w_router": nrm(ks[16], (DEPTH, D, N_EXPERTS), D),
        "moe_bias": rnd(ks[17], (DEPTH, N_EXPERTS), 0.01),
        "moe_w1": nrm(ks[18], (DEPTH, N_EXPERTS, D, EXPERT_FF), D),
        "moe_w3": nrm(ks[19], (DEPTH, N_EXPERTS, D, EXPERT_FF), D),
        "moe_w2": nrm(ks[20], (DEPTH, N_EXPERTS, EXPERT_FF, D), EXPERT_FF),
        "sh_w1": nrm(ks[21], (DEPTH, D, SHARED_FF), D),
        "sh_w3": nrm(ks[22], (DEPTH, D, SHARED_FF), D),
        "sh_w2": nrm(ks[23], (DEPTH, SHARED_FF, D), SHARED_FF),
        "final_g": 1.0 + rnd(ks[24], (D,), 0.05),
    }

def reference(x, c, ada_w, ada_b, norm1_g, norm2_g, ev_w_in, ev_dw_w, ev_dw_b, ev_ln_g, ev_ln_b,
              ev_w_out, od_w_in, od_w_grp, od_scale, od_w_out, moe_w_router, moe_bias, moe_w1,
              moe_w3, moe_w2, sh_w1, sh_w3, sh_w2, final_g):
    cond = jax.nn.silu(c)
    for l in range(DEPTH):
        mod = cond @ ada_w[l] + ada_b[l]
        sh1, sc1, g1, sh2, sc2, g2 = [m[:, None, :] for m in jnp.split(mod, 6, axis=-1)]
        h = modulate(rmsnorm(x, norm1_g[l]), sh1, sc1)
        i = l // 2
        if l % 2 == 0:
            y = even_mixer(h, ev_w_in[i], ev_dw_w[i], ev_dw_b[i], ev_ln_g[i], ev_ln_b[i], ev_w_out[i])
        else:
            y = odd_mixer(h, od_w_in[i], od_w_grp[i], od_scale[i], od_w_out[i])
        x = x + g1 * y
        h = modulate(rmsnorm(x, norm2_g[l]), sh2, sc2)
        x = x + g2 * moe_ffn(h, moe_w_router[l], moe_bias[l], moe_w1[l], moe_w3[l], moe_w2[l],
                             sh_w1[l], sh_w3[l], sh_w2[l])
    return rmsnorm(x, final_g)


_drawn_inputs = setup_inputs


def setup_inputs(seed=0):
    import zlib

    import numpy as np

    out = dict(_drawn_inputs(seed))
    spreads = {}
    factors = {'norm1_g': 2.785, 'ev_dw_b': 5.718, 'ev_ln_g': 4.267, 'ev_ln_b': 19.397}
    for name, (base, spread) in spreads.items():
        noise = np.random.default_rng([zlib.crc32(name.encode()), seed]).standard_normal(out[name].shape)
        drawn = base * np.exp(spread * noise) if base else spread * noise
        out[name] = __import__('jax').numpy.asarray(drawn.astype(out[name].dtype))
    for name, factor in factors.items():
        out[name] = (out[name] * factor).astype(out[name].dtype)
    return out
```

```python
from contextlib import ExitStack

import concourse.bass as bass
from concourse import mybir

F32 = mybir.dt.float32
F32R = mybir.dt.float32r
I32 = mybir.dt.int32
ALU = mybir.AluOpType
ACT = mybir.ActivationFunctionType
AX_X = mybir.AxisListType.X

P = 128
D = 1024
T = 256
TC = T // P
KD = D // P
HEADS, DH = 8, 64
SBW = HEADS * DH
CW = D // 2
TAPS = 31
PADC = TAPS - 1
MC = CW // P
WINDOWS = (2, 4, 8, 16)
PADP = 16
E = 64
GROUPS, PER = 8, 8
TOPG = 4
FF = 256
ROUTED_SCALE = 2.5
EPS = 1e-6
BIG = 1e30
BLK = 64
NBLK = T // BLK
PAIRS = E // 2
ADA = 6 * D
UNIT = 2048
NSLOT = 12
UC = UNIT // KD
ADAC = ADA // PAIRS
HB = 256
TW = P + 4
LIST = 64

V_C, V_G1, V_G2, V_OS, V_DW, V_DB, V_LG, V_LB, V_N = 0, 8, 24, 40, 48, 172, 176, 180, 184


class Chain:

    def __init__(self, eng, sem):
        self.eng, self.sem, self.n = eng, sem, 0

    def step(self, ins):
        ins.then_inc(self.sem, 1)
        self.n += 1
        return self.n

    def wait(self, upto=None):
        self.eng.wait_ge(self.sem, self.n if upto is None else upto)


def trunk(nc, x_d, vec_d, ada_w, ada_b, ev_w_in, ev_w_out, od_w_in, od_w_grp, od_w_out,
          w_router, moe_bias, w1, w3, w2, s1, s3, s2, final_g, out_d):
    with ExitStack() as ctx:
        def sb(name, shape, dt=F32, where=ctx):
            return where.enter_context(nc.sbuf_tensor(name, shape, dt))

        def sem(name):
            return ctx.enter_context(nc.semaphore(name))

        PS = ctx.enter_context(nc.psum_tensor("PS", [P, 8, 512], F32))
        ring = sb("ring", [P, NSLOT, UNIT])
        x = sb("x", [P, TC, D])
        xn = sb("xn", [P, TC, D])
        hT = sb("hT", [P, KD, T])
        gates = sb("gates", [P, 2, D])
        acc = sb("acc", [P, ADA])
        vec = sb("vec", [P, V_N])
        cond = sb("cond", [P, KD])
        eps = sb("eps", [P, 1])
        stat = sb("stat", [P, 4])
        scl = sb("scl", [P, 2, KD])
        shf = sb("shf", [P, 2, KD])
        wr = sb("wr", [P, KD, E])
        biasr = sb("biasr", [P, 2, E])
        ident = sb("ident", [P, P])
        suffix = sb("suffix", [P, P])
        before = sb("before", [P, P])
        ones = sb("ones", [P, P])
        slotno = sb("slotno", [P, E])
        idcol = sb("idcol", [P, 2, 4])
        blkno = sb("blkno", [P, 4])
        lower = sb("lower", [P, GROUPS, GROUPS])
        twice = sb("twice", [P, LIST])
        mixer = ExitStack()
        mixT = sb("mixT", [P, KD, T], where=mixer)
        work = ExitStack()
        qT = sb("qT", [P, SBW // P, T], where=work)
        kT = sb("kT", [P, SBW // P, T], where=work)
        v = sb("v", [P, TC, SBW], where=work)
        zs = sb("zs", [P, 4, 384], where=work)
        lg = sb("lg", [P, 4, 384], where=work)
        mask = sb("mask", [P, 384], where=work)
        negmask = sb("negmask", [P, 384], where=work)
        u = sb("u", [P, MC, PADC + T], where=work)
        sig = sb("sig", [P, MC, T], where=work)
        cv = sb("cv", [P, MC, T], where=work)
        mean_w = sb("mean_w", [P, P], where=work)
        work.close()
        up = sb("up", [P, KD, PADP + T], where=mixer)
        pooled = sb("pooled", [P, KD, T], where=mixer)
        win = sb("win", [P, 4, PADP + T], where=mixer)
        icnt = sb("icnt", [P, PADP], where=mixer)
        fix = sb("fix", [P, PADP], where=mixer)
        mixer.close()
        xh = sb("xh", [P, TC, KD, P], F32R)
        xl = sb("xl", [P, TC, KD, P], F32R)
        adab1 = sb("adab1", [P, KD * ADAC])
        adab = [hT[:].rearrange("p k t -> p (k t)")[:, 0:KD * ADAC], adab1[:]]
        adat = sb("adat", [P, ADAC])
        xg = xn[:].rearrange("p b (k s) -> p b k s", s=P)
        hot = sb("hot", [P, 2, TC, P], F32R)
        idw = sb("idw", [P, 2, TC, TW], F32R)
        hotT = sb("hotT", [P, TC, TW], F32R)
        wslot = sb("wslot", [P, 1])
        hsil = sb("hsil", [P, 2, 2 * BLK])
        hid = sb("hid", [P, 2, 2, BLK])
        yh = sb("yh", [P, D], F32R)
        yl = sb("yl", [P, D], F32R)
        shs = xn[:, 1, 0:512]
        shid = hT[:].rearrange("p k t -> p (k t)")[:, KD * ADAC:KD * ADAC + 2 * T].rearrange("p (m t) -> p m t", m=2)
        sc = sb("sc", [P, TC, E])
        bz = sb("bz", [P, TC, E])
        bz2 = sb("bz2", [P, TC, E])
        sel = sb("sel", [P, TC, E])
        wts = sb("wts", [P, TC, E])
        wsp = sb("wsp", [P, TC, 2, E], F32R)
        top = sb("top", [P, TC * GROUPS, 8])
        gsc = sb("gsc", [P, TC * GROUPS])
        gcmp = sb("gcmp", [P, TC * GROUPS, GROUPS])
        geq = sb("geq", [P, TC * GROUPS, GROUPS])
        grank = sb("grank", [P, TC * GROUPS])
        goff = sb("goff", [P, TC * GROUPS])
        t8 = sb("t8", [P, TC, 8])
        wsum = sb("wsum", [P, TC])
        where = sb("where", [P, TC, 1 + NBLK * E])
        need = sb("need", [P, 8])
        rank = sb("rank", [P, 4])
        pick = sb("pick", [P, 3, LIST])
        ctlf = sb("ctlf", [P, 2 * LIST + 1])
        ctl = sb("ctl", [P, 2 * LIST + 1], I32)

        x_landed = sem("x_landed")
        small_landed = sem("small_landed")
        bias_landed = [sem(f"bias_landed{l}") for l in range(2)]
        landed = [sem(f"landed{s}") for s in range(NSLOT)]
        adab_landed = [sem(f"adab_landed{s}") for s in range(2)]
        consts = sem("consts")
        acc_zeroed = sem("acc_zeroed")
        pool_consts = sem("pool_consts")
        pool_const = sem("pool_const")
        dve_step = sem("dve_step")
        act_step = sem("act_step")
        eps_ready = sem("eps_ready")
        cond_ready = sem("cond_ready")
        ada_used = sem("ada_used")
        ada_step = sem("ada_step")
        adab_used = sem("adab_used")
        rms_ready = sem("rms_ready")
        xn_ready = sem("xn_ready")
        xT_filled = sem("xT_filled")
        hT_ready = sem("hT_ready")
        split_ready = sem("split_ready")
        params_filled = sem("params_filled")
        params_ready = sem("params_ready")
        gate_filled = sem("gate_filled")
        gate_ready = sem("gate_ready")
        final_landed = sem("final_landed")
        router_landed = sem("router_landed")
        out_used = sem("out_used")
        shared_used = sem("shared_used")
        proj_filled = sem("proj_filled")
        proj_taken = sem("proj_taken")
        conv_in = sem("conv_in")
        conv_done = sem("conv_done")
        conv_copied = sem("conv_copied")
        ln_filled = sem("ln_filled")
        centred = sem("centred")
        squared = sem("squared")
        ln_root = sem("ln_root")
        ln_ready = sem("ln_ready")
        conv_mix = sem("conv_mix")
        z_filled = sem("z_filled")
        z_taken = sem("z_taken")
        softplus_ready = sem("softplus_ready")
        logm_ready = sem("logm_ready")
        suffix_filled = sem("suffix_filled")
        suffix_taken = sem("suffix_taken")
        exp_ready = sem("exp_ready")
        probs_ready = sem("probs_ready")
        att_filled = sem("att_filled")
        att_taken = sem("att_taken")
        pool_in = sem("pool_in")
        pooled_ready = sem("pooled_ready")
        grp_filled = sem("grp_filled")
        grp_taken = sem("grp_taken")
        out_filled = sem("out_filled")
        logits_filled = sem("logits_filled")
        scores_ready = sem("scores_ready")
        sel_ready = sem("sel_ready")
        pos_filled = sem("pos_filled")
        need_ready = sem("need_ready")
        rank_filled = sem("rank_filled")
        pick_ready = sem("pick_ready")
        list_filled = sem("list_filled")
        ctl_ready = sem("ctl_ready")
        shared_filled = sem("shared_filled")
        shared_silu = sem("shared_silu")
        shared_hidden = sem("shared_hidden")
        stored = sem("stored")

        class Flow:

            def __init__(self, tag):
                self.base = 0
                self.hot_ready = sem(f"{tag}_hot_ready")
                self.gather_filled = sem(f"{tag}_gather_filled")
                self.gather_taken = sem(f"{tag}_gather_taken")
                self.turn_filled = sem(f"{tag}_turn_filled")
                self.turn_taken = sem(f"{tag}_turn_taken")
                self.up_filled = sem(f"{tag}_up_filled")
                self.silu_ready = sem(f"{tag}_silu_ready")
                self.hidden_ready = sem(f"{tag}_hidden_ready")
                self.down_used = sem(f"{tag}_down_used")
                self.down_filled = sem(f"{tag}_down_filled")
                self.y_high = sem(f"{tag}_y_high")
                self.y_split = sem(f"{tag}_y_split")
                self.slotw_ready = sem(f"{tag}_slotw_ready")
                self.scattered = sem(f"{tag}_scattered")

        main = [Flow(f"main{l}") for l in range(2)]
        more = [Flow(f"more{l}") for l in range(2)]
        more_free = [sem(f"more{l}_free") for l in range(2)]
        more_landed = [[sem(f"more{l}_landed{s}") for s in range(6)] for l in range(2)]

        PIECES = ([("gate", m) for m in range(4)] + [("val", m) for m in range(4)]
                  + [("v", i) for i in range(4)] + [("k", m) for m in range(4)] + [("q", m) for m in range(4)])
        NACT_EVEN = 16

        even_units = ([("ada", 0, i) for i in range(8)] + [("in", 0, i) for i in (8, 9, 6, 7, 4, 5, 2, 3, 0, 1)]
                      + [("ada", 0, i) for i in range(8, 24)] + [("out", 0, i) for i in range(4)]
                      + [("shared", 0, i) for i in range(3)])
        odd_units = ([("in", 1, i) for i in range(4)] + [("grp", 1, 0)] + [("out", 1, i) for i in range(4)]
                     + [("shared", 1, i) for i in range(3)])
        first_slot = [(-len(even_units)) % NSLOT, 6]
        occupant = [None] * NSLOT
        uses = [0] * NSLOT
        schedule = []
        at = {}

        def last_use(unit, position):
            kind, l, i = unit
            if kind == "ada":
                return ada_used, i + 1
            if kind == "in":
                return proj_filled, len(PIECES) * l + 2 * (position + 1)
            if kind == "grp":
                return grp_filled, KD
            if kind == "out":
                return (out_used, 3 * l + i + 1) if i < 3 else (out_filled, 4 * (l + 1))
            return (shared_filled, l + 1) if i == 1 else (shared_used, 2 * l + 1 + i // 2)

        expert_uses = []
        for l, units in enumerate((even_units, odd_units)):
            rows, ins_seen = [], 0
            for n, unit in enumerate(units):
                s = (first_slot[l] + n) % NSLOT
                uses[s] += 1
                rows.append((unit, s, 16 * uses[s], occupant[s]))
                at[unit] = (s, 16 * uses[s])
                occupant[s] = last_use(unit, ins_seen)
                ins_seen += unit[0] == "in"
            schedule.append(rows)
            expert_uses.append(list(uses))
            before_experts = list(occupant)
            rows.append(before_experts)
            for s in range(NSLOT):
                uses[s] += PAIRS // 2
                occupant[s] = "more" if s < 6 else (main[l].down_filled, main[l].base + PAIRS)

        def unit_source(unit):
            kind, l, i = unit
            if kind == "ada":
                return ada_w[l].rearrange("(p k) n -> p k n", k=KD)[:, :, i * UC:(i + 1) * UC]
            if kind == "in":
                w = ev_w_in if l == 0 else od_w_in
                return w.rearrange("(p k) n -> p k n", k=KD)[:, :, i * UC:(i + 1) * UC]
            if kind == "out":
                w = ev_w_out if l == 0 else od_w_out
                return w.rearrange("(i r p) n -> i p r n", r=2, p=P)[i]
            if kind == "grp":
                return od_w_grp.rearrange("g (r p) n -> p (g r) n", p=P)
            return (s1, s3, s2)[i][l].rearrange("(p k) n -> p (k n)", p=P)

        def slot_view(s, rows):
            return ring[:, s, :].rearrange("p (k n) -> p k n", k=rows)

        def piece_bank(i):
            return PS[:, (0, 1, 5, 6)[i % 4], 0:T]

        block = ctx.enter_context(nc.Block())

        @block.sync
        def _(sp):
            sp.dma_start(x[:], x_d.rearrange("(c p) d -> p c d", p=P)).then_inc(x_landed, 16)

            last_trips = []

            def wait_occupant(who):
                if who == "more":
                    sp.wait_ge(more[0].down_filled, last_trips[0])
                elif who is not None:
                    sp.wait_ge(*who)

            def load_expert(l, e, j, it=None, static_prev=None):
                for i, w in enumerate((w1, w3, w2)):
                    s = 3 * j + i
                    if static_prev is not None:
                        wait_occupant(static_prev[s])
                    else:
                        f = main[l]
                        if i < 2:
                            sp.wait_ge(f.up_filled, e + (2 * f.base - 3))
                        else:
                            sp.wait_ge(f.down_filled if j % 2 else f.down_used, it * 2 + (f.base - 1 + j // 2))
                    sp.dma_start(ring[:, s, :], w[l, bass.ds(e, 1)].rearrange("o (p k) n -> p (o k n)", p=P)
                                 ).then_inc(landed[s], 16)

            def load_ada_next(pair, par, first):
                if not first:
                    sp.wait_ge(adab_used, pair - 1)
                sp.dma_start(adab[par].rearrange("p (k n) -> p k n", k=KD),
                             ada_w[1].rearrange("(p k) n -> p k n", k=KD)[:, :, bass.ds(pair * ADAC, ADAC)]
                             ).then_inc(adab_landed[par], 16)

            for l in range(2):
                rows = schedule[l]
                for unit, s, _, who in rows[:-1]:
                    wait_occupant(who)
                    dst = ring[:, s, :] if unit[0] == "shared" else slot_view(s, 2 if unit[0] == "out" else KD)
                    sp.dma_start(dst, unit_source(unit)).then_inc(landed[s], 16)
                prev = rows[-1]
                for j in range(4):
                    load_expert(l, j, j, static_prev=prev)
                if l == 0:
                    sp.wait_ge(split_ready, 1)
                    sp.wait_ge(shared_filled, 1)
                    for j in range(2):
                        load_ada_next(j, j, True)
                with sp.Fori(1, PAIRS // 2) as it:
                    for j in range(4):
                        load_expert(l, it * 4 + j, j, it)
                        if l == 0 and j % 2 == 1:
                            load_ada_next(it * 2 + j // 2, j // 2, False)
                f = main[l]
                sp.wait_ge(ctl_ready, l + 1)
                trips = sp.value_load(ctl[0:1, 0:1], min_val=1, max_val=LIST // 2)
                last_trips.append(trips)
                with sp.Fori(0, trips) as i:
                    for j in range(2):
                        e = sp.value_load(ctl[0:1, bass.ds(i * 2 + (1 + LIST + j), 1)], min_val=0, max_val=E - 1)
                        if j == 0:
                            sp.wait_ge(more_free[l], i + 1)
                        for n, w in enumerate((w1, w3, w2)):
                            sp.dma_start(ring[:, 3 * j + n, :],
                                         w[l, bass.ds(e, 1)].rearrange("o (p k) n -> p (o k n)", p=P)
                                         ).then_inc(more_landed[l][3 * j + n], 16)
            sp.wait_ge(stored, 16 * TC)

        @block.gpsimd
        def _(pool):
            made = [0]

            def const(ins):
                ins.then_inc(pool_const, 1)
                made[0] += 1
                pool.wait_ge(pool_const, made[0])

            def put(dst, cmp, base, pattern, mult, fill=0.0):
                const(nc.gpsimd.affine_select(out=dst, in_=dst, compare_op=cmp, fill=fill, base=base,
                                              pattern=pattern, channel_multiplier=mult))

            nc.gpsimd.memset(acc[:], 0.0).then_inc(acc_zeroed, 1)
            nc.gpsimd.memset(eps[:], EPS).then_inc(eps_ready, 1)
            const(nc.gpsimd.memset(ident[:], 0.0))
            put(ident[:], ALU.not_equal, 0, [[-1, P]], 1, 1.0)
            const(nc.gpsimd.memset(suffix[:], 1.0))
            put(suffix[:], ALU.is_ge, 0, [[-1, P]], 1)
            const(nc.gpsimd.memset(before[:], 1.0))
            put(before[:], ALU.is_gt, 0, [[1, P]], -1)
            const(nc.gpsimd.memset(ones[:], 1.0))
            const(nc.gpsimd.memset(mean_w[:], 1.0 / CW))
            const(nc.gpsimd.memset(mask[:], 1.0))
            put(mask[:, 0:P], ALU.is_gt, 0, [[1, P]], -1)
            put(mask[:, 2 * P:3 * P], ALU.is_gt, 0, [[1, P]], -1)
            const(nc.gpsimd.memset(negmask[:], -1.0))
            put(negmask[:, 0:P], ALU.is_gt, 0, [[1, P]], -1)
            put(negmask[:, 2 * P:3 * P], ALU.is_gt, 0, [[1, P]], -1)
            const(nc.gpsimd.memset(u[:, :, 0:PADC], 0.0))
            const(nc.gpsimd.iota(slotno[:], pattern=[[1, E]], base=0, channel_multiplier=0,
                                allow_small_or_imprecise_dtypes=True))
            const(nc.gpsimd.iota(twice[:], pattern=[[2, LIST]], base=0, channel_multiplier=0,
                                allow_small_or_imprecise_dtypes=True))
            const(nc.gpsimd.iota(idcol[:, 0, :], pattern=[[0, 4]], base=0, channel_multiplier=1,
                                allow_small_or_imprecise_dtypes=True))
            const(nc.gpsimd.iota(idcol[:, 1, :], pattern=[[E, 4]], base=1 + E, channel_multiplier=1,
                                allow_small_or_imprecise_dtypes=True))
            const(nc.gpsimd.iota(blkno[:], pattern=[[BLK, 4]], base=BLK, channel_multiplier=0,
                                allow_small_or_imprecise_dtypes=True))
            const(nc.gpsimd.memset(lower[:], 1.0))
            nc.gpsimd.affine_select(out=lower[:], in_=lower[:], compare_op=ALU.is_gt, fill=0.0, base=0,
                                    pattern=[[1, GROUPS], [-1, GROUPS]], channel_multiplier=0).then_inc(consts, 1)
            pool.wait_ge(params_ready, 2)
            pool.wait_ge(gate_ready, 2)
            nc.gpsimd.memset(acc[:], 0.0).then_inc(acc_zeroed, 1)
            pool.wait_ge(acc_zeroed, 2)
            pool.dma_start(acc[0:1, :], ada_b[1:2, :]).then_inc(bias_landed[1], 16)
            pool.wait_ge(logits_filled, 1)
            pool.dma_start(wr[:].rearrange("p k e -> p (k e)"),
                           w_router[1].rearrange("(p k) e -> p (k e)", k=KD)).then_inc(router_landed, 16)
            pool.wait_ge(params_ready, 3)
            nc.gpsimd.memset(up[:, :, 0:PADP], 0.0)
            nc.gpsimd.iota(icnt[:], pattern=[[1, PADP]], base=1, channel_multiplier=0,
                                allow_small_or_imprecise_dtypes=True).then_inc(pool_consts, 1)
            pool.wait_ge(gate_ready, 4)
            pool.dma_start(acc[:, 0:D], final_g[0].partition_broadcast(P)).then_inc(final_landed, 16)

        @block.scalar
        def _(act):
            SMALL = 4
            act.dma_start(vec[:], vec_d).then_inc(small_landed, 16)
            act.dma_start(wr[:].rearrange("p k e -> p (k e)"),
                          w_router[0].rearrange("(p k) e -> p (k e)", k=KD)).then_inc(small_landed, 16)
            for l in range(2):
                act.dma_start(biasr[:, l, :], moe_bias[l].partition_broadcast(P)).then_inc(small_landed, 16)
            act.wait_ge(acc_zeroed, 1)
            act.dma_start(acc[0:1, :], ada_b[0:1, :]).then_inc(bias_landed[0], 16)
            own = Chain(act, act_step)

            def square_sums(n):
                if n == 0:
                    act.wait_ge(x_landed, 16)
                for c in range(TC):
                    ins = nc.scalar.activation(xn[:, c, :], x[:, c, :], ACT.Square, scale=float(D) ** -0.5,
                                               accum_out=stat[:, c:c + 1])
                    own.step(ins)
                own.wait()
                nc.scalar.activation(stat[:, 2:4], stat[:, 0:2], ACT.Sqrt, bias=eps[:, 0:1]).then_inc(rms_ready, 1)

            def modulate(n):
                if n == 0:
                    act.wait_ge(params_ready, 1)
                else:
                    act.wait_ge(params_ready, n + 1)
                for k in range(KD):
                    act.wait_ge(xT_filled, KD * n + 2 * (k // 2) + 2)
                    nc.scalar.activation(hT[:, k, :], PS[:, k // 2, (k % 2) * HB:(k % 2) * HB + HB], ACT.Identity,
                                         scale=scl[:, n % 2, k:k + 1], bias=shf[:, n % 2, k:k + 1]
                                         ).then_inc(hT_ready, 1)

            def copy_gates(l):
                for g in range(2):
                    act.wait_ge(gate_filled, 2 * l + g + 1)
                    nc.scalar.copy(gates[:, g, :].rearrange("p (b n) -> p b n", b=2), PS[:, 5:7, :]
                                   ).then_inc(gate_ready, 1)

            act.wait_ge(small_landed, 16 * SMALL)
            nc.scalar.activation(cond[:], vec[:, V_C:V_C + KD], ACT.Silu).then_inc(cond_ready, 1)
            act.wait_ge(eps_ready, 1)
            square_sums(0)
            modulate(0)

            for i, (kind, m) in enumerate(PIECES):
                if kind == "val":
                    continue
                act.wait_ge(proj_filled, i + 1)
                if kind == "gate":
                    ins = nc.scalar.activation(sig[:, m, :], piece_bank(i), ACT.Sigmoid)
                elif kind == "v":
                    ins = nc.scalar.copy(v[:, m % 2, (m // 2) * UC:(m // 2) * UC + UC], piece_bank(i))
                elif kind == "k":
                    ins = nc.scalar.copy(kT[:, m, :], piece_bank(i))
                else:
                    ins = nc.scalar.mul(qT[:, m, :], piece_bank(i), DH ** -0.5)
                ins.then_inc(proj_taken, 1)
            for b in range(2):
                if b:
                    act.wait_ge(att_filled, 2)
                for hh in range(4):
                    h = 4 * b + hh
                    act.wait_ge(z_filled, h + 1)
                    own.step(nc.scalar.activation(lg[:, hh, :], PS[:, 5 + h % 2, 0:384], ACT.Abs))
                    nc.scalar.copy(zs[:, hh, :], PS[:, 5 + h % 2, 0:384]).then_inc(z_taken, 1)
                own.wait()
                own.step(nc.scalar.activation(lg[:], lg[:], ACT.Exp, scale=-1.0))
                own.wait()
                nc.scalar.activation(lg[:], lg[:], ACT.Ln, bias=1.0).then_inc(softplus_ready, 1)
                act.wait_ge(suffix_taken, 4 * b + 4)
                nc.scalar.activation(zs[:], zs[:], ACT.Exp).then_inc(exp_ready, 1)
                for j in range(2 * b, 2 * b + 2):
                    act.wait_ge(att_filled, j + 1)
                    nc.scalar.copy(mixT[:, j, :], PS[:, 7, 0:T]).then_inc(att_taken, 1)
            act.wait_ge(conv_done, MC)
            nc.scalar.copy(cv[:].rearrange("p (b m) t -> p b (m t)", b=2), PS[:, 2:4, :]).then_inc(conv_copied, 1)
            act.wait_ge(centred, 1)
            nc.scalar.activation(cv[:], sig[:], ACT.Square).then_inc(squared, 1)
            act.wait_ge(ln_filled, 2)
            nc.scalar.activation(PS[:, 6, HB:2 * HB], PS[:, 6, 0:T], ACT.Sqrt, bias=eps[:, 0:1]).then_inc(ln_root, 1)
            act.wait_ge(ln_ready, 1)
            for m in range(MC):
                nc.scalar.activation(mixT[:, 4 + m, :], sig[:, m, :], ACT.Silu, scale=vec[:, V_LG + m:V_LG + m + 1],
                                     bias=vec[:, V_LB + m:V_LB + m + 1]).then_inc(conv_mix, 1)

            def gather_out(f, pr, par, j):
                act.wait_ge(f.gather_filled, (pr + f.base) * 2 + (j + 1))
                for k in range(4 * j, 4 * j + 4):
                    ins = nc.scalar.activation(xg[:, par, k, :], PS[:, 7, (k % 4) * P:(k % 4 + 1) * P],
                                               ACT.Identity, scale=scl[:, 1, k:k + 1], bias=shf[:, 1, k:k + 1])
                ins.then_inc(f.gather_taken, 1)

            def silu_half(f, pr, hf):
                act.wait_ge(f.up_filled, (pr + f.base) * 2 + (hf + 1))
                nc.scalar.activation(hsil[:, hf, :], PS[:, 6, 0:2 * BLK], ACT.Silu).then_inc(f.silu_ready, 1)

            def turn_out(f, pr):
                act.wait_ge(f.turn_filled, pr + (f.base + 1))
                nc.scalar.copy(hotT[:], PS[:, 7, :].rearrange("p (c n) -> p c n", c=TC)[:, :, 0:TW]
                               ).then_inc(f.turn_taken, 1)

            def y_high(f, pr):
                act.wait_ge(f.down_filled, pr + (f.base + 1))
                act.wait_ge(f.slotw_ready, pr + (f.base + 1))
                nc.scalar.activation(yh[:].rearrange("p (b n) -> p b n", b=2), PS[:, 4:6, :], ACT.Copy,
                                     scale=wslot[:, 0:1]).then_inc(f.y_high, 1)

            def moe(l):
                square_sums(2 * l + 1)
                modulate(2 * l + 1)
                act.wait_ge(logits_filled, l + 1)
                nc.scalar.activation(sc[:], PS[:, 6, 0:TC * E].rearrange("p (c e) -> p c e", c=TC), ACT.Sigmoid
                                     ).then_inc(scores_ready, 1)
                act.wait_ge(shared_filled, l + 1)
                nc.scalar.activation(shs, PS[:, 4, :], ACT.Silu).then_inc(shared_silu, 1)
                f = main[l]
                for j in range(2):
                    gather_out(f, 0, 0, j)

                def pair(pr, par, last=False):
                    silu_half(f, pr, 0)
                    if not last:
                        gather_out(f, pr + 1, 1 - par, 0)
                    silu_half(f, pr, 1)
                    if not last:
                        gather_out(f, pr + 1, 1 - par, 1)
                    turn_out(f, pr)
                    y_high(f, pr)

                with act.Fori(0, PAIRS // 2 - 1) as it:
                    for par in range(2):
                        pair(it * 2 + par, par)
                pair(PAIRS - 2, 0)
                pair(PAIRS - 1, 1, last=True)
                g = more[l]
                act.wait_ge(ctl_ready, l + 1)
                trips = act.value_load(ctl[0:1, 0:1], min_val=1, max_val=LIST // 2)
                with act.Fori(0, trips) as i:
                    for j in range(2):
                        gather_out(g, i, 0, j)
                    silu_half(g, i, 0)
                    silu_half(g, i, 1)
                    turn_out(g, i)
                    y_high(g, i)

            copy_gates(0)
            act.wait_ge(xn_ready, 2)
            moe(0)

            act.wait_ge(xn_ready, 4)
            square_sums(2)
            modulate(2)
            for i in range(KD):
                act.wait_ge(proj_filled, len(PIECES) + i + 1)
                if i == 0:
                    act.wait_ge(pool_consts, 1)
                nc.scalar.copy(up[:, i, PADP:], piece_bank(i)).then_inc(proj_taken, 1)
            for i in range(KD):
                act.wait_ge(grp_filled, i + 1)
                nc.scalar.activation(mixT[:, i, :], piece_bank(i), ACT.Copy, scale=vec[:, V_OS + i:V_OS + i + 1]
                                     ).then_inc(grp_taken, 1)
            copy_gates(1)
            act.wait_ge(xn_ready, 6)
            moe(1)
            act.wait_ge(xn_ready, 8)
            square_sums(4)
            for c in range(TC):
                act.wait_ge(xn_ready, 9 + c)
                act.dma_start(out_d[c * P:(c + 1) * P, :], x[:, c, :]).then_inc(stored, 16)

        @block.vector
        def _(dve):
            own = Chain(dve, dve_step)
            V = nc.vector

            def scale_x(n):
                dve.wait_ge(rms_ready, n + 1)
                own.step(V.reciprocal(stat[:, 0:2], stat[:, 2:4]))
                own.wait()
                if n < 4:
                    for c in range(TC):
                        ins = V.tensor_scalar(xn[:, c, :], x[:, c, :], stat[:, c:c + 1], None, ALU.mult)
                    ins.then_inc(xn_ready, 1)

            def split_x(l):
                for c in range(TC):
                    src = x[:, c, :].rearrange("p (q k) -> p k q", k=KD)
                    own.step(V.tensor_scalar(xh[:, c, :, :], src, stat[:, c:c + 1], None, ALU.mult))
                    own.wait()
                    ins = V.scalar_tensor_tensor(out=xl[:, c, :, :], in0=src, scalar=stat[:, c:c + 1],
                                                 in1=xh[:, c, :, :].bitcast(F32), op0=ALU.mult, op1=ALU.subtract)
                ins.then_inc(split_ready, 1)

            def fold_ada(i):
                s, n = at[("ada", 0, i)]
                dve.wait_ge(landed[s], n)
                wv = slot_view(s, KD)
                cols = acc[:, i * UC:(i + 1) * UC]
                part = PS[:, 4, (i % 2) * HB:(i % 2) * HB + UC]
                if i >= 2:
                    dve.wait_ge(ada_used, i - 1)
                for k in range(KD):
                    if k:
                        own.wait()
                    ins = V.scalar_tensor_tensor(
                        out=cols if k == KD - 1 else part, in0=wv[:, k, :], scalar=cond[:, k:k + 1],
                        in1=cols if k == 0 else part, op0=ALU.mult, op1=ALU.add)
                    if k < KD - 1:
                        own.step(ins)
                ins.then_inc(ada_used, 1)

            def params(l, which):
                dve.wait_ge(params_filled, 2 * l + which + 1)
                gain = V_G1 if which == 0 else V_G2
                V.tensor_copy(shf[:, which, :], PS[:, 7, 0:KD])
                V.scalar_tensor_tensor(out=scl[:, which, :], in0=PS[:, 7, KD:2 * KD], scalar=1.0,
                                       in1=vec[:, gain + l * KD:gain + (l + 1) * KD], op0=ALU.add, op1=ALU.mult
                                       ).then_inc(params_ready, 1)

            def residual(l, which):
                dve.wait_ge(gate_ready, 2 * l + which + 1)
                for c in range(TC):
                    for h in range(2):
                        b = 2 * c + h
                        if which == 0:
                            dve.wait_ge(out_filled, 4 * l + b + 1)
                        cols = slice(h * 512, (h + 1) * 512)
                        own.step(V.tensor_tensor(xn[:, c, cols], PS[:, b, :], gates[:, which, cols], ALU.mult))
                for c in range(TC):
                    for h in range(2):
                        cols = slice(h * 512, (h + 1) * 512)
                        own.wait(own.n if (c, h) == (1, 1) else own.n - 3 + 2 * c + h)
                        ins = V.tensor_tensor(x[:, c, cols], x[:, c, cols], xn[:, c, cols], ALU.add)
                ins.then_inc(xn_ready, 1)

            def route(l):
                dve.wait_ge(scores_ready, l + 1)
                own.step(V.tensor_tensor(bz[:], sc[:], biasr[:, l:l + 1, :].to_broadcast([P, TC, E]), ALU.add))
                own.wait()
                for c in range(TC):
                    for g in range(GROUPS):
                        ins = V.max(top[:, c * GROUPS + g, :], bz[:, c, g * PER:(g + 1) * PER])
                own.step(ins)
                own.wait()
                own.step(V.tensor_tensor(gsc[:], top[:, :, 0], top[:, :, 1], ALU.add))
                own.wait()
                for c in range(TC):
                    cs = slice(c * GROUPS, (c + 1) * GROUPS)
                    other = gsc[:, cs].unsqueeze(1).to_broadcast([P, GROUPS, GROUPS])
                    self_ = gsc[:, cs].unsqueeze(2).to_broadcast([P, GROUPS, GROUPS])
                    own.step(V.tensor_tensor(gcmp[:, cs, :], other, self_, ALU.is_gt))
                    own.step(V.tensor_tensor(geq[:, cs, :], other, self_, ALU.is_equal))
                    own.wait()
                    own.step(V.tensor_tensor(geq[:, cs, :], geq[:, cs, :], lower[:], ALU.mult))
                own.wait()
                own.step(V.tensor_tensor(gcmp[:], gcmp[:], geq[:], ALU.add))
                own.wait()
                own.step(V.tensor_reduce(grank[:], gcmp[:], AX_X, ALU.add))
                own.wait()
                own.step(V.tensor_scalar(grank[:], grank[:], TOPG - 0.5, None, ALU.is_lt))
                own.wait()
                own.step(V.tensor_scalar(goff[:], grank[:], BIG, -BIG, ALU.mult, ALU.add))
                own.wait()
                by_group = [P, TC * GROUPS, PER]
                bz_g = bz[:].rearrange("p c (g e) -> p (c g) e", e=PER)
                own.step(V.tensor_tensor(bz_g, bz_g, grank[:].unsqueeze(2).to_broadcast(by_group), ALU.mult))
                own.wait()
                own.step(V.tensor_tensor(bz_g, bz_g, goff[:].unsqueeze(2).to_broadcast(by_group), ALU.add))
                own.wait()
                for c in range(TC):
                    own.step(V.max(t8[:, c, :], bz[:, c, :]))
                own.wait()
                for c in range(TC):
                    own.step(V.match_replace(bz2[:, c, :], t8[:, c, :], bz[:, c, :], -3e38))
                own.wait()
                V.tensor_tensor(sel[:], bz[:], bz2[:], ALU.not_equal).then_inc(sel_ready, 1)
                dve.wait_ge(sel_ready, l + 1)
                own.step(V.tensor_tensor(wts[:], sel[:], sc[:], ALU.mult))
                own.wait()
                own.step(V.tensor_reduce(wsum[:], wts[:], AX_X, ALU.add))
                own.wait()
                own.step(V.reciprocal(wsum[:], wsum[:]))
                own.wait()
                for c in range(TC):
                    own.step(V.tensor_scalar(wts[:, c, :], wts[:, c, :], wsum[:, c:c + 1], ROUTED_SCALE,
                                             ALU.mult, ALU.mult))
                own.wait()
                own.step(V.tensor_copy(wsp[:, :, 0, :], wts[:]))
                own.wait()
                own.step(V.tensor_tensor(wsp[:, :, 1, :], wts[:], wsp[:, :, 0, :].bitcast(F32), ALU.subtract))
                dve.wait_ge(pos_filled, l + 1)
                w0 = where[:, :, 1:1 + E]
                own.step(V.scalar_tensor_tensor(out=w0, in0=PS[:, 6, HB:HB + TC * E].rearrange("p (c e) -> p c e", c=TC),
                                                scalar=1.0, in1=sel[:], op0=ALU.add, op1=ALU.mult))
                own.step(V.memset(where[:, :, 0:1], -1.0))
                own.wait()
                own.step(V.tensor_scalar(w0, w0, -1.0, None, ALU.add))
                own.wait()

            def block_list(l):
                own.step(V.tensor_copy(need[0:E, 6:7], PS[0:E, 6, HB + P:HB + P + 1]))
                for b in range(1, NBLK):
                    own.step(V.tensor_scalar(where[:, :, 1 + b * E:1 + (b + 1) * E], where[:, :, 1:1 + E],
                                             -float(BLK * b), None, ALU.add))
                own.wait()
                own.step(V.tensor_scalar(need[0:E, 0:3], blkno[0:E, 0:3], need[0:E, 6:7], None, ALU.is_lt))
                own.step(V.memset(need[0:E, 3:4], 0.0))
                own.wait()
                own.step(V.tensor_copy(need[0:E, 4:5], need[0:E, 0:1]))
                V.tensor_tensor(need[0:E, 5:6], need[0:E, 0:1], need[0:E, 1:2], ALU.add).then_inc(need_ready, 1)
                dve.wait_ge(rank_filled, l + 1)
                own.step(V.scalar_tensor_tensor(out=rank[0:E, 0:3], in0=PS[0:E, 4, 0:3], scalar=1.0,
                                                in1=need[0:E, 0:3], op0=ALU.add, op1=ALU.mult))
                own.wait()
                own.step(V.tensor_scalar(rank[0:E, 0:3], rank[0:E, 0:3], -1.0, None, ALU.add))
                own.wait()
                for b in range(3):
                    ins = V.tensor_scalar(pick[0:E, b, :], slotno[0:E, :], rank[0:E, b:b + 1], None, ALU.is_equal)
                ins.then_inc(pick_ready, 1)
                dve.wait_ge(list_filled, l + 1)
                own.step(V.tensor_reduce(ctlf[0:1, 0:1], PS[0:1, 4, 256:259], AX_X, ALU.add))
                own.wait()
                own.step(V.tensor_scalar(ctlf[0:1, 1:1 + LIST], twice[0:1, :], ctlf[0:1, 0:1], None, ALU.is_lt))
                own.wait()
                own.step(V.tensor_reduce(ctlf[0:1, 0:1], ctlf[0:1, 1:1 + LIST], AX_X, ALU.add))
                own.wait()
                own.step(V.tensor_scalar(ctl[0:1, 0:1], ctlf[0:1, 0:1], 1.0, None, ALU.max))
                V.tensor_copy(ctl[0:1, 1:1 + 2 * LIST], PS[0:1, 4, 8:8 + 2 * LIST]).then_inc(ctl_ready, 1)

            def one_hot(f, pr, par, wait_turn):
                if wait_turn:
                    dve.wait_ge(f.turn_filled, pr + (f.base - 1))
                for c in range(TC):
                    for hf in range(2):
                        V.tensor_scalar(hot[:, par, c, hf * BLK:(hf + 1) * BLK], slotno[:],
                                        where[:, c, bass.ds(pr * 2 + (1 + hf), 1)], None, ALU.is_equal)
                for c in range(TC):
                    ins = V.tensor_copy(idw[:, par, c, P:TW].rearrange("p (s e) -> p s e", s=2),
                                        wsp[:, c, :, bass.ds(pr * 2, 2)].bitcast(F32))
                ins.then_inc(f.hot_ready, 1)

            def one_hot_more(f, i, par):
                for hf in range(2):
                    code = dve.value_load(ctl[0:1, bass.ds(i * 2 + (1 + hf), 1)], min_val=0, max_val=NBLK * E)
                    e = dve.value_load(ctl[0:1, bass.ds(i * 2 + (1 + LIST + hf), 1)], min_val=0, max_val=E - 1)
                    for c in range(TC):
                        V.tensor_scalar(hot[:, par, c, hf * BLK:(hf + 1) * BLK], slotno[:],
                                        where[:, c, bass.ds(code, 1)], None, ALU.is_equal)
                        ins = V.tensor_copy(idw[:, par, c, P:TW].rearrange("p (s e) -> p s e", s=2)[:, :, hf:hf + 1],
                                            wsp[:, c, :, bass.ds(e, 1)].bitcast(F32))
                ins.then_inc(f.hot_ready, 1)

            def hidden(f, pr, hf):
                dve.wait_ge(f.silu_ready, (pr + f.base) * 2 + (hf + 1))
                V.tensor_tensor(hid[:, hf, :, :].rearrange("p m t -> p (m t)"), PS[:, 6, 2 * BLK:4 * BLK],
                                hsil[:, hf, :], ALU.mult).then_inc(f.hidden_ready, 1)

            def slot_weights(f, pr):
                dve.wait_ge(f.turn_taken, pr + (f.base + 1))
                for hf in range(2):
                    rows = slice(hf * BLK, (hf + 1) * BLK)
                    parts = hotT[rows, :, P + hf:TW:2].bitcast(F32)
                    ins = V.tensor_reduce(wslot[rows, :], parts, mybir.AxisListType.XY, ALU.add)
                ins.then_inc(f.slotw_ready, 1)

            def y_low(f, pr):
                dve.wait_ge(f.y_high, pr + (f.base + 1))
                V.scalar_tensor_tensor(out=yl[:].rearrange("p (b n) -> p b n", b=2), in0=PS[:, 4:6, :],
                                       scalar=wslot[:, 0:1], in1=yh[:].bitcast(F32).rearrange("p (b n) -> p b n", b=2),
                                       op0=ALU.mult, op1=ALU.subtract).then_inc(f.y_split, 1)

            def fold_ada_next(pr, par):
                dve.wait_ge(adab_landed[par], (pr - par) * 8 + 16)
                wv = adab[par].rearrange("p (k n) -> p k n", k=KD)
                cols = acc[:, bass.ds(pr * ADAC, ADAC)]
                for k in range(KD):
                    if k:
                        dve.wait_ge(ada_step, pr * (KD - 1) + k)
                    ins = V.scalar_tensor_tensor(out=cols if k == KD - 1 else adat[:], in0=wv[:, k, :],
                                                 scalar=cond[:, k:k + 1], in1=cols if k == 0 else adat[:],
                                                 op0=ALU.mult, op1=ALU.add)
                    ins.then_inc(ada_step if k < KD - 1 else adab_used, 1)

            def moe(l):
                f = main[l]
                scale_x(2 * l + 1)
                split_x(l)
                if l == 0:
                    dve.wait_ge(consts, 1)
                for par in range(2):
                    for c in range(TC):
                        own.step(V.tensor_copy(idw[:, par, c, 0:P], ident[:]))
                route(l)
                one_hot(f, 0, 0, False)
                one_hot(f, 1, 1, False)
                dve.wait_ge(shared_silu, l + 1)
                V.tensor_tensor(shid.rearrange("p m t -> p (m t)"), PS[:, 5, :], shs, ALU.mult
                                ).then_inc(shared_hidden, 1)
                block_list(l)

                def pair(pr, par, more_to_come=True):
                    hidden(f, pr, 0)
                    hidden(f, pr, 1)
                    if l == 0:
                        fold_ada_next(pr, par)
                    slot_weights(f, pr)
                    if more_to_come:
                        one_hot(f, pr + 2, par, True)
                    y_low(f, pr)

                if l == 0:
                    dve.wait_ge(bias_landed[1], 16)
                with dve.Fori(0, PAIRS // 2 - 1) as it:
                    for par in range(2):
                        pair(it * 2 + par, par)
                pair(PAIRS - 2, 0, False)
                pair(PAIRS - 1, 1, False)
                g = more[l]
                trips = dve.value_load(ctl[0:1, 0:1], min_val=1, max_val=LIST // 2)
                dve.wait_ge(f.turn_filled, PAIRS + f.base)
                with dve.Fori(0, trips) as i:
                    one_hot_more(g, i, 0)
                    hidden(g, i, 0)
                    hidden(g, i, 1)
                    slot_weights(g, i)
                    y_low(g, i)
                    dve.wait_ge(g.scattered, i + 1)
                residual(l, 1)

            scale_x(0)
            dve.wait_ge(cond_ready, 1)
            dve.wait_ge(bias_landed[0], 16)
            for i in range(8):
                fold_ada(i)
            params(0, 0)
            for m in range(MC):
                dve.wait_ge(proj_taken, m + 1)
                dve.wait_ge(proj_filled, 4 + m + 1)
                V.tensor_tensor(u[:, m, PADC:], piece_bank(4 + m), sig[:, m, :], ALU.mult).then_inc(conv_in, 1)
            dve.wait_ge(conv_in, MC)

            def conv_tap(j):
                for m in range(MC):
                    y = PS[:, 2 + m // 2, (m % 2) * HB:(m % 2) * HB + HB]
                    tap = vec[:, V_DW + m * TAPS + j:V_DW + m * TAPS + j + 1]
                    if j == 0:
                        own.step(V.tensor_scalar(y, u[:, m, 0:T], tap, vec[:, V_DB + m:V_DB + m + 1], ALU.mult, ALU.add))
                    else:
                        own.wait(taps_at[m])
                        ins = V.scalar_tensor_tensor(out=y, in0=u[:, m, j:j + T], scalar=tap, in1=y,
                                                     op0=ALU.mult, op1=ALU.add)
                        if j == TAPS - 1:
                            ins.then_inc(conv_done, 1)
                            continue
                        own.step(ins)
                    taps_at[m] = own.n

            taps_at = [0] * MC

            def attention(b):
                dve.wait_ge(softplus_ready, b + 1)
                own.step(V.scalar_tensor_tensor(out=lg[:], in0=zs[:], scalar=0.0, in1=lg[:], op0=ALU.max, op1=ALU.add))
                own.wait()
                V.tensor_tensor(lg[:], lg[:], negmask[:].unsqueeze(1).to_broadcast([P, 4, 384]), ALU.mult
                                ).then_inc(logm_ready, 1)
                for hh in range(4):
                    h = 4 * b + hh
                    dve.wait_ge(suffix_filled, h + 1)
                    V.tensor_tensor(zs[:, hh, :], zs[:, hh, :], PS[:, h % 2, 0:384], ALU.add).then_inc(suffix_taken, 1)
                dve.wait_ge(exp_ready, b + 1)
                V.scalar_tensor_tensor(out=zs[:], in0=zs[:], scalar=1.0,
                                       in1=mask[:].unsqueeze(1).to_broadcast([P, 4, 384]),
                                       op0=ALU.min, op1=ALU.mult).then_inc(probs_ready, 1)

            i = 8
            for j in range(TAPS):
                conv_tap(j)
                if j % 3 == 2 and i < 16:
                    fold_ada(i)
                    i += 1
            attention(0)
            while i < 24:
                if i == 20:
                    attention(1)
                fold_ada(i)
                i += 1
            dve.wait_ge(ln_filled, 1)
            dve.wait_ge(conv_copied, 1)
            V.tensor_tensor(sig[:], cv[:], PS[:, 5, 0:T].unsqueeze(1).to_broadcast([P, MC, T]), ALU.subtract
                            ).then_inc(centred, 1)
            dve.wait_ge(ln_root, 1)
            own.step(V.reciprocal(PS[:, 4, HB:2 * HB], PS[:, 6, HB:2 * HB]))
            own.wait()
            dve.wait_ge(squared, 1)
            V.tensor_tensor(sig[:], sig[:], PS[:, 4, HB:2 * HB].unsqueeze(1).to_broadcast([P, MC, T]), ALU.mult
                            ).then_inc(ln_ready, 1)
            params(0, 1)
            residual(0, 0)
            moe(0)

            scale_x(2)
            params(1, 0)
            dve.wait_ge(pool_consts, 1)
            own.step(V.reciprocal(icnt[:], icnt[:]))
            for m in range(KD):
                g = m // 2
                dve.wait_ge(proj_taken, NACT_EVEN + m + 1)
                src, step = up[:, m, :], 1
                for n in range(g + 1):
                    lo = 1 if n == 0 else 2 ** (n + 1)
                    own.step(V.tensor_tensor(win[:, n, lo:], src[:, lo:], src[:, lo - step:PADP + T - step], ALU.add))
                    own.wait()
                    src, step = win[:, n, :], 2 * step
                w = WINDOWS[g]
                own.step(V.scalar_tensor_tensor(out=pooled[:, m, :], in0=src[:, PADP:], scalar=1.0 / w,
                                                in1=up[:, m, PADP:], op0=ALU.mult, op1=ALU.subtract))
                own.step(V.tensor_tensor(fix[:, 0:w], src[:, PADP:PADP + w], icnt[:, 0:w], ALU.mult))
                own.wait()
                V.tensor_tensor(pooled[:, m, 0:w], fix[:, 0:w], up[:, m, PADP:PADP + w], ALU.subtract
                                ).then_inc(pooled_ready, 1)
            params(1, 1)
            residual(1, 0)
            moe(1)
            dve.wait_ge(final_landed, 16)
            scale_x(4)
            for c in range(TC):
                own.step(V.tensor_scalar(xn[:, c, :], x[:, c, :], stat[:, c:c + 1], None, ALU.mult))
                own.wait()
                V.tensor_tensor(x[:, c, :], xn[:, c, :], acc[:, 0:D], ALU.mult).then_inc(xn_ready, 1)

        @block.tensor
        def _(pe):
            M = nc.tensor.matmul

            def transposes(n):
                pe.wait_ge(xn_ready, 2 * n + 1)
                if n == 0:
                    pe.wait_ge(consts, 1)
                for k in range(KD):
                    for c in range(TC):
                        o = (k % 2) * HB + c * P
                        ins = nc.tensor.transpose(PS[:, k // 2, o:o + P], xn[:, c, k::KD], ident[:])
                    ins.then_inc(xT_filled, 1)

            def param_columns(l, which):
                for s in range(2):
                    sec = 3 * which + s
                    for k in range(KD):
                        ins = M(PS[:, 7, s * KD + k:s * KD + k + 1], acc[:, sec * D + k:(sec + 1) * D:KD],
                                ones[:, 0:1], start=True, stop=True)
                ins.then_inc(params_filled, 1)

            def gate_rows(l):
                for g in range(2):
                    if g:
                        pe.wait_ge(gate_ready, 2 * l + 1)
                    for h in range(2):
                        o = (2 + 3 * g) * D + h * 512
                        ins = M(PS[:, 5 + h, :], ones[:], acc[:, o:o + 512], start=True, stop=True)
                    ins.then_inc(gate_filled, 1)

            def landed_wait(unit):
                s, n = at[unit]
                pe.wait_ge(landed[s], n)
                return s

            def project(n, l, units, pieces, taken):
                pe.wait_ge(hT_ready, KD * (n + 1))
                for i, (unit, kind, sub) in enumerate(pieces):
                    s = landed_wait(unit)
                    wv = slot_view(s, KD)
                    if i >= 4:
                        taken(i - 4)
                    for k in range(KD):
                        if kind == "v":
                            ins = M(piece_bank(i), hT[:, k, sub * P:(sub + 1) * P], wv[:, k, :],
                                    start=(k == 0), stop=(k == KD - 1))
                        else:
                            ins = M(piece_bank(i), wv[:, k, sub * P:(sub + 1) * P], hT[:, k, :],
                                    start=(k == 0), stop=(k == KD - 1))
                    ins.then_inc(proj_filled, 1)

            def output(l, ready):
                for i in range(4):
                    s = landed_wait(("out", l, i))
                    wv = slot_view(s, 2)
                    for r in range(2):
                        kk = 2 * i + r
                        ready(kk)
                        for c in range(TC):
                            for h in range(2):
                                ins = M(PS[:, 2 * c + h, :], mixT[:, kk, c * P:(c + 1) * P],
                                        wv[:, r, h * 512:(h + 1) * 512], start=(kk == 0), stop=(kk == KD - 1))
                                if kk == KD - 1:
                                    ins.then_inc(out_filled, 1)
                    if i < 3:
                        ins.then_inc(out_used, 1)

            def gather(f, par, j, bank_free):
                if bank_free:
                    pe.wait_ge(*bank_free)
                for k in range(4 * j, 4 * j + 4):
                    o, n = (k % 4) * P, 0
                    for c in range(TC):
                        for part in (xh, xl):
                            ins = M(PS[:, 7, o:o + P], part[:, c, k, :], hot[:, par, c, :],
                                    start=(n == 0), stop=(n == 3))
                            n += 1
                ins.then_inc(f.gather_filled, 1)

            def up(f, par, hf, slots, bank_free):
                if bank_free:
                    pe.wait_ge(*bank_free)
                for j in range(2):
                    s, sm, val = slots[j]
                    pe.wait_ge(sm, val)
                    wv = slot_view(s, KD)
                    for m in range(2):
                        o = j * 2 * BLK + m * BLK
                        for k in range(KD):
                            ins = M(PS[:, 6, o:o + BLK], wv[:, k, m::2], xg[:, par, k, hf * BLK:(hf + 1) * BLK],
                                    start=(k == 0), stop=(k == KD - 1))
                ins.then_inc(f.up_filled, 1)

            def turn(f, par, gather_at):
                pe.wait_ge(f.gather_taken, gather_at)
                for c in range(TC):
                    ins = M(PS[:, 7, c * HB:c * HB + TW], hot[:, par, c, :], idw[:, par, c, :],
                            start=True, stop=True)
                ins.then_inc(f.turn_filled, 1)

            def down(f, hf, slot, hidden_at, freed=None):
                pe.wait_ge(f.hidden_ready, hidden_at)
                s, sm, val = slot
                pe.wait_ge(sm, val)
                wv = slot_view(s, 2)
                for h in range(2):
                    for j in range(2):
                        ins = M(PS[hf * BLK:(hf + 1) * BLK, 4 + h, :], hid[:, hf, j, :],
                                wv[:, j, h * 512:(h + 1) * 512], start=(j == 0), stop=(j == 1))
                        if freed is not None and h == j == 0:
                            ins.then_inc(freed, 1)
                return ins

            def scatter(f, split_at, freed=None):
                pe.wait_ge(f.y_split, split_at)
                for c in range(TC):
                    for h in range(2):
                        for part in (yh, yl):
                            ins = M(PS[:, 2 * c + h, :], hotT[:, c, 0:P], part[:, h * 512:(h + 1) * 512],
                                    start=False, stop=False, skip_group_check=True)
                            if freed is not None:
                                ins.then_inc(freed, 1)
                                freed = None
                ins.then_inc(f.scattered, 1)

            def moe(l):
                n = 2 * l + 1
                transposes(n)
                pe.wait_ge(hT_ready, KD * (n + 1))
                if l == 0:
                    pe.wait_ge(small_landed, 16 * 4)
                else:
                    pe.wait_ge(router_landed, 16)
                for c in range(TC):
                    for k in range(KD):
                        ins = M(PS[:, 6, c * E:(c + 1) * E], hT[:, k, c * P:(c + 1) * P], wr[:, k, :],
                                start=(k == 0), stop=(k == KD - 1))
                ins.then_inc(logits_filled, 1)
                for j in range(2):
                    s = landed_wait(("shared", l, j))
                    wv = slot_view(s, KD)
                    for m in range(2):
                        for k in range(KD):
                            ins = M(PS[:, 4 + j, m * HB:(m + 1) * HB], wv[:, k, m::2], hT[:, k, :],
                                    start=(k == 0), stop=(k == KD - 1))
                    if j == 0:
                        ins.then_inc(shared_used, 1)
                ins.then_inc(shared_filled, 1)
                pe.wait_ge(sel_ready, l + 1)
                pe.wait_ge(scores_ready, l + 1)
                for c in range(TC):
                    o = PS[:, 6, HB + c * E:HB + (c + 1) * E]
                    if c:
                        M(o, ones[:], sel[:, 0, :], start=True, stop=False)
                    M(o, before[:], sel[:, c, :], start=(c == 0), stop=True)
                for c in range(TC):
                    ins = M(PS[0:E, 6, HB + P:HB + P + 1], sel[:, c, :], ones[:, 0:1],
                            start=(c == 0), stop=(c == TC - 1))
                ins.then_inc(pos_filled, 1)
                f = main[l]
                B = f.base
                pe.wait_ge(f.hot_ready, B + 1)
                pe.wait_ge(split_ready, l + 1)
                for j in range(2):
                    gather(f, 0, j, (f.gather_taken, 2 * B + 1) if j else None)
                pe.wait_ge(shared_hidden, l + 1)
                s = landed_wait(("shared", l, 2))
                wv = slot_view(s, 2)
                for c in range(TC):
                    for h in range(2):
                        for j in range(2):
                            ins = M(PS[:, 2 * c + h, :], shid[:, j, c * P:(c + 1) * P],
                                    wv[:, j, h * 512:(h + 1) * 512], start=(j == 0), stop=(j == 1))
                ins.then_inc(shared_used, 1)
                pe.wait_ge(need_ready, l + 1)
                M(PS[0:E, 4, 0:3], before[0:E, 0:E], need[0:E, 0:3], start=True, stop=False)
                M(PS[0:E, 4, 0:3], ones[0:E, 0:E], need[0:E, 3:6], start=False, stop=True).then_inc(rank_filled, 1)
                pe.wait_ge(pick_ready, l + 1)
                for t in range(2):
                    for b in range(3):
                        M(PS[0:1, 4, 8 + t * LIST:8 + (t + 1) * LIST], idcol[0:E, 1 - t, b:b + 1], pick[0:E, b, :],
                          start=(b == 0), stop=(b == 2))
                M(PS[0:1, 4, 256:259], ones[0:E, 0:1], need[0:E, 0:3], start=True, stop=True).then_inc(list_filled, 1)

                def pair(pr, par, first=False, last=False):
                    def slot(hf, i):
                        s = 6 * par + 3 * hf + i
                        return s, landed[s], (pr - par) * 8 + (16 * expert_uses[l][s] + 16)
                    q = pr + B
                    pe.wait_ge(f.gather_taken, q * 2 + 2)
                    up(f, par, 0, (slot(0, 0), slot(0, 1)), None if first else (f.hidden_ready, q * 2))
                    if not first:
                        scatter(f, q)
                    if not last:
                        pe.wait_ge(f.hot_ready, q + 2)
                        gather(f, 1 - par, 0, None if first else (f.turn_taken, q))
                    up(f, par, 1, (slot(1, 0), slot(1, 1)), (f.hidden_ready, q * 2 + 1))
                    if not last:
                        gather(f, 1 - par, 1, (f.gather_taken, q * 2 + 3))
                    if first:
                        pe.wait_ge(ctl_ready, l + 1)
                    down(f, 0, slot(0, 2), q * 2 + 1, more_free[l] if last else None).then_inc(f.down_used, 1)
                    if last:
                        pe.wait_ge(f.turn_taken, q)
                    turn(f, par, q * 2 + (2 if last else 4))
                    down(f, 1, slot(1, 2), q * 2 + 2).then_inc(f.down_filled, 1)

                pair(0, 0, first=True)
                pair(1, 1)
                with pe.Fori(1, PAIRS // 2 - 1) as it:
                    for par in range(2):
                        pair(it * 2 + par, par)
                pair(PAIRS - 2, 0)
                pair(PAIRS - 1, 1, last=True)
                scatter(f, B + PAIRS)

                g = more[l]
                trips = pe.value_load(ctl[0:1, 0:1], min_val=1, max_val=LIST // 2)
                pe.wait_ge(f.turn_taken, B + PAIRS)
                pe.wait_ge(f.hidden_ready, 2 * (B + PAIRS))
                with pe.Fori(0, trips) as i:
                    def slot(hf, n):
                        return 3 * hf + n, more_landed[l][3 * hf + n], i * 16 + 16
                    pe.wait_ge(g.hot_ready, i + 1)
                    for j in range(2):
                        gather(g, 0, j, (g.gather_taken, i * 2 + 1) if j else None)
                    pe.wait_ge(g.gather_taken, i * 2 + 2)
                    up(g, 0, 0, (slot(0, 0), slot(0, 1)), None)
                    up(g, 0, 1, (slot(1, 0), slot(1, 1)), (g.hidden_ready, i * 2 + 1))
                    turn(g, 0, i * 2 + 2)
                    down(g, 0, slot(0, 2), i * 2 + 1).then_inc(g.down_used, 1)
                    down(g, 1, slot(1, 2), i * 2 + 2).then_inc(g.down_filled, 1)
                    scatter(g, i + 1, more_free[l])

            transposes(0)
            pe.wait_ge(ada_used, 8)
            param_columns(0, 0)
            pieces = [(("in", 0, 8 + m // 2), "col", m % 2) for m in range(4)]
            pieces += [(("in", 0, 6 + m // 2), "col", m % 2) for m in range(4)]
            pieces += [(("in", 0, 4 + i // 2), "v", i % 2) for i in range(4)]
            pieces += [(("in", 0, 2 + m // 2), "col", m % 2) for m in range(4)]
            pieces += [(("in", 0, m // 2), "col", m % 2) for m in range(4)]

            def even_taken(i):
                if 4 <= i < 8:
                    pe.wait_ge(conv_in, i - 3)
                else:
                    pe.wait_ge(proj_taken, i + 1 if i < 4 else i - 3)

            project(0, 0, None, pieces, even_taken)
            pe.wait_ge(proj_taken, NACT_EVEN)
            for b in range(2):
                for h in range(4 * b, 4 * b + 4):
                    if h >= 2:
                        pe.wait_ge(z_taken, h - 1)
                    rows = slice(DH * (h % 2), DH * (h % 2) + DH)
                    M(PS[:, 5 + h % 2, 0:T], kT[rows, h // 2, 0:P], qT[rows, h // 2, :], start=True, stop=True)
                    M(PS[:, 5 + h % 2, T:T + P], kT[rows, h // 2, P:T], qT[rows, h // 2, P:T],
                      start=True, stop=True).then_inc(z_filled, 1)
                pe.wait_ge(logm_ready, b + 1)
                for h in range(4 * b, 4 * b + 4):
                    hh = h % 4
                    if h >= 2:
                        pe.wait_ge(suffix_taken, h - 1)
                    o = PS[:, h % 2, :]
                    M(o[:, 0:T], suffix[:], lg[:, hh, 0:T], start=True, stop=False)
                    M(o[:, P:T], ones[:], lg[:, hh, T:T + P], start=False, stop=True)
                    M(o[:, T:T + P], suffix[:], lg[:, hh, T:T + P], start=True, stop=True).then_inc(suffix_filled, 1)
                pe.wait_ge(probs_ready, b + 1)
                for h in range(4 * b, 4 * b + 4):
                    hh, j = h % 4, h // 2
                    if j and h % 2 == 0:
                        pe.wait_ge(att_taken, j)
                    o = PS[DH * (h % 2):DH * (h % 2) + DH, 7, 0:T]
                    M(o, v[:, 0, h * DH:(h + 1) * DH], zs[:, hh, 0:T], start=True, stop=False)
                    ins = M(o[:, P:T], v[:, 1, h * DH:(h + 1) * DH], zs[:, hh, T:T + P], start=False, stop=True)
                    if h % 2:
                        ins.then_inc(att_filled, 1)
            pe.wait_ge(conv_copied, 1)
            for m in range(MC):
                ins = M(PS[:, 5, 0:T], mean_w[:], cv[:, m, :], start=(m == 0), stop=(m == MC - 1))
            ins.then_inc(ln_filled, 1)
            pe.wait_ge(squared, 1)
            for m in range(MC):
                ins = M(PS[:, 6, 0:T], mean_w[:], cv[:, m, :], start=(m == 0), stop=(m == MC - 1))
            ins.then_inc(ln_filled, 1)
            pe.wait_ge(ada_used, 24)
            pe.wait_ge(att_taken, 4)
            param_columns(0, 1)
            pe.wait_ge(ln_ready, 1)
            gate_rows(0)

            def even_ready(kk):
                if kk >= 4:
                    pe.wait_ge(conv_mix, kk - 3)

            output(0, even_ready)
            moe(0)

            pe.wait_ge(adab_used, PAIRS)
            param_columns(1, 0)
            transposes(2)

            def odd_taken(i):
                pe.wait_ge(proj_taken, NACT_EVEN + i + 1)

            project(2, 1, None, [(("in", 1, m // 2), "col", m % 2) for m in range(KD)], odd_taken)
            s = landed_wait(("grp", 1, 0))
            wv = slot_view(s, KD)
            for i in range(KD):
                g, n = i // 2, i % 2
                pe.wait_ge(pooled_ready, 2 * g + 2)
                pe.wait_ge(proj_taken, NACT_EVEN + KD)
                if i >= 4:
                    pe.wait_ge(grp_taken, i - 3)
                for r in range(2):
                    ins = M(piece_bank(i), wv[:, 2 * g + r, n * P:(n + 1) * P], pooled[:, 2 * g + r, :],
                            start=(r == 0), stop=(r == 1))
                ins.then_inc(grp_filled, 1)
            pe.wait_ge(params_ready, 3)
            param_columns(1, 1)
            pe.wait_ge(grp_taken, KD)
            gate_rows(1)
            output(1, lambda kk: None)
            moe(1)


_NAMES = ["x", "vec", "ada_w", "ada_b", "ev_w_in", "ev_w_out", "od_w_in", "od_w_grp", "od_w_out",
          "moe_w_router", "moe_bias", "moe_w1", "moe_w3", "moe_w2", "sh_w1", "sh_w3", "sh_w2", "final_g"]


def kernel(**inputs):
    import numpy as np
    import concourse.bacc as bacc
    from concourse.bass_utils import run_bass_kernel_spmd as run

    a = {n: np.ascontiguousarray(inputs[n]) for n in inputs}
    by_row = lambda w: w.reshape(P, KD)
    by_chunk = lambda w: w.reshape(-1, P).T
    cols = [by_row(a["c"][0])] + [by_row(a["norm1_g"][l]) for l in range(2)]
    cols += [by_row(a["norm2_g"][l]) for l in range(2)] + [by_chunk(a["od_scale"][0])]
    cols += [a["ev_dw_w"][0, :, 0, :].reshape(TAPS, MC, P).transpose(2, 1, 0).reshape(P, MC * TAPS)]
    cols += [by_chunk(a[n][0]) for n in ("ev_dw_b", "ev_ln_g", "ev_ln_b")]
    a["vec"] = np.ascontiguousarray(np.concatenate(cols, axis=1))
    a["x"] = a["x"][0]
    for n in ("ev_w_in", "ev_w_out", "od_w_in", "od_w_grp", "od_w_out"):
        a[n] = a[n][0]
    a["final_g"] = a["final_g"].reshape(1, D)

    nc = bacc.Bacc("TRN2", target_bir_lowering=False, num_devices=1)
    arrays, args = {}, []
    for name in _NAMES:
        arrays[f"in_{name}"] = np.ascontiguousarray(a[name])
        args.append(nc.dram_tensor(f"in_{name}", a[name].shape, mybir.dt.from_np(a[name].dtype),
                                   kind="ExternalInput").ap())
    args.append(nc.dram_tensor("out", (T, D), F32, kind="ExternalOutput").ap())
    trunk(nc, *args)
    r = run(nc, [arrays], core_ids=[0])
    return r.results[0]["out"].reshape(inputs["x"].shape)
```

```python
from contextlib import ExitStack

import concourse.bass as bass
from concourse import mybir

F32 = mybir.dt.float32
F32R = mybir.dt.float32r
I32 = mybir.dt.int32
ALU = mybir.AluOpType
ACT = mybir.ActivationFunctionType
AX_X = mybir.AxisListType.X

P = 128
D = 1024
T = 256
TC = T // P
KD = D // P
HEADS, DH = 8, 64
SBW = HEADS * DH
CW = D // 2
TAPS = 31
PADC = TAPS - 1
MC = CW // P
WINDOWS = (2, 4, 8, 16)
PADP = 16
E = 64
GROUPS, PER = 8, 8
TOPG = 4
FF = 256
ROUTED_SCALE = 2.5
EPS = 1e-6
BIG = 1e30
BLK = 64
NBLK = T // BLK
PAIRS = E // 2
ADA = 6 * D
UNIT = 2048
NSLOT = 12
UC = UNIT // KD
ADAC = ADA // PAIRS
HB = 256
TW = P + 4
LOG0 = 23
LIST = 64

V_C, V_G1, V_G2, V_OS, V_DW, V_DB, V_LG, V_LB, V_N = 0, 8, 24, 40, 48, 172, 176, 180, 184


class Chain:

    def __init__(self, eng, sem):
        self.eng, self.sem, self.n = eng, sem, 0

    def step(self, ins):
        ins.then_inc(self.sem, 1)
        self.n += 1
        return self.n

    def wait(self, upto=None):
        self.eng.wait_ge(self.sem, self.n if upto is None else upto)


def trunk(nc, x_d, vec_d, ada_w, ada_b, ev_w_in, ev_w_out, od_w_in, od_w_grp, od_w_out,
          w_router, moe_bias, w1, w3, w2, s1, s3, s2, final_g, out_d):
    with ExitStack() as ctx:
        def sb(name, shape, dt=F32, where=ctx):
            return where.enter_context(nc.sbuf_tensor(name, shape, dt))

        def sem(name):
            return ctx.enter_context(nc.semaphore(name))

        PS = ctx.enter_context(nc.psum_tensor("PS", [P, 8, 512], F32))
        ring = sb("ring", [P, NSLOT, UNIT])
        x = sb("x", [P, TC, D])
        xn = sb("xn", [P, TC, D])
        hT = sb("hT", [P, KD, T])
        gates = sb("gates", [P, 2, D])
        acc = sb("acc", [P, ADA])
        vec = sb("vec", [P, V_N])
        cond = sb("cond", [P, KD])
        eps = sb("eps", [P, 1])
        stat = sb("stat", [P, 4])
        scl = sb("scl", [P, 2, KD])
        shf = sb("shf", [P, 2, KD])
        wr = sb("wr", [P, KD, E])
        biasr = sb("biasr", [P, 2, E])
        ident = sb("ident", [P, P])
        suffix = sb("suffix", [P, P])
        before = sb("before", [P, P])
        ones = sb("ones", [P, P])
        slotno = sb("slotno", [P, E])
        idcol = sb("idcol", [P, 2, 4])
        blkno = sb("blkno", [P, 4])
        lower = sb("lower", [P, GROUPS, GROUPS])
        mixer = ExitStack()
        mixT = sb("mixT", [P, KD, T], where=mixer)
        work = ExitStack()
        qT = sb("qT", [P, SBW // P, T], where=work)
        kT = sb("kT", [P, SBW // P, T], where=work)
        v = sb("v", [P, TC, SBW], where=work)
        zs = sb("zs", [P, 4, 384], where=work)
        lg = sb("lg", [P, 4, 384], where=work)
        mask = sb("mask", [P, 384], where=work)
        negmask = sb("negmask", [P, 384], where=work)
        u = sb("u", [P, MC, PADC + T], where=work)
        sig = sb("sig", [P, MC, T], where=work)
        cv = sb("cv", [P, MC, T], where=work)
        mean_w = sb("mean_w", [P, P], where=work)
        work.close()
        up = sb("up", [P, KD, PADP + T], where=mixer)
        pooled = sb("pooled", [P, KD, T], where=mixer)
        win = sb("win", [P, 4, PADP + T], where=mixer)
        icnt = sb("icnt", [P, PADP], where=mixer)
        fix = sb("fix", [P, PADP], where=mixer)
        mixer.close()
        xh = sb("xh", [P, TC, KD, P], F32R)
        xl = sb("xl", [P, TC, KD, P], F32R)
        adab1 = sb("adab1", [P, KD * ADAC])
        adab = [hT[:].rearrange("p k t -> p (k t)")[:, 0:KD * ADAC], adab1[:]]
        adat = sb("adat", [P, ADAC])
        xg = xn[:].rearrange("p b (k s) -> p b k s", s=P)
        hot = sb("hot", [P, 2, TC, P], F32R)
        idw = sb("idw", [P, 2, TC, TW], F32R)
        hotT = sb("hotT", [P, TC, TW], F32R)
        wslot = sb("wslot", [P, 1])
        hid = sb("hid", [P, FF])
        hidT = sb("hidT", [P, 2, P])
        yh = sb("yh", [P, D], F32R)
        yl = sb("yl", [P, D], F32R)
        shs = xn[:, 1, 0:512]
        shid = hT[:].rearrange("p k t -> p (k t)")[:, KD * ADAC:KD * ADAC + 2 * T].rearrange("p (m t) -> p m t", m=2)
        sc = sb("sc", [P, TC, E])
        bz = sb("bz", [P, TC, E])
        bz2 = sb("bz2", [P, TC, E])
        sel = sb("sel", [P, TC, E])
        wts = sb("wts", [P, TC, E])
        wsp = sb("wsp", [P, TC, 2, E], F32R)
        top = sb("top", [P, TC * GROUPS, 8])
        gsc = sb("gsc", [P, TC * GROUPS])
        gcmp = sb("gcmp", [P, TC * GROUPS, GROUPS])
        geq = sb("geq", [P, TC * GROUPS, GROUPS])
        grank = sb("grank", [P, TC * GROUPS])
        goff = sb("goff", [P, TC * GROUPS])
        t8 = sb("t8", [P, TC, 8])
        wsum = sb("wsum", [P, TC])
        where = sb("where", [P, TC, 1 + NBLK * E])
        need = sb("need", [P, 8])
        rank = sb("rank", [P, 4])
        pick = sb("pick", [P, 3, LIST])
        ctlf = sb("ctlf", [P, 2 * LIST + 1])
        ctl = sb("ctl", [P, 2 * LIST + 1], I32)

        x_landed = sem("x_landed")
        small_landed = sem("small_landed")
        bias_landed = [sem(f"bias_landed{l}") for l in range(2)]
        landed = [sem(f"landed{s}") for s in range(NSLOT)]
        adab_landed = [sem(f"adab_landed{s}") for s in range(2)]
        consts = sem("consts")
        acc_zeroed = sem("acc_zeroed")
        pool_consts = sem("pool_consts")
        pool_const = sem("pool_const")
        dve_step = sem("dve_step")
        act_step = sem("act_step")
        eps_ready = sem("eps_ready")
        cond_ready = sem("cond_ready")
        ada_used = sem("ada_used")
        ada_row_filled = sem("ada_row_filled")
        ada_row_added = sem("ada_row_added")
        ada_step = sem("ada_step")
        adab_used = sem("adab_used")
        rms_ready = sem("rms_ready")
        xn_ready = sem("xn_ready")
        xT_filled = sem("xT_filled")
        hT_ready = sem("hT_ready")
        split_ready = sem("split_ready")
        params_filled = sem("params_filled")
        params_ready = sem("params_ready")
        gate_filled = sem("gate_filled")
        gate_ready = sem("gate_ready")
        final_landed = sem("final_landed")
        router_landed = sem("router_landed")
        out_used = sem("out_used")
        shared_used = sem("shared_used")
        proj_filled = sem("proj_filled")
        proj_taken = sem("proj_taken")
        conv_in = sem("conv_in")
        conv_done = sem("conv_done")
        conv_copied = sem("conv_copied")
        ln_filled = sem("ln_filled")
        centred = sem("centred")
        squared = sem("squared")
        ln_root = sem("ln_root")
        ln_ready = sem("ln_ready")
        conv_mix = sem("conv_mix")
        z_filled = sem("z_filled")
        z_taken = sem("z_taken")
        softplus_ready = sem("softplus_ready")
        logm_ready = sem("logm_ready")
        suffix_filled = sem("suffix_filled")
        suffix_taken = sem("suffix_taken")
        exp_ready = sem("exp_ready")
        probs_ready = sem("probs_ready")
        att_filled = sem("att_filled")
        att_taken = sem("att_taken")
        pool_in = sem("pool_in")
        pooled_ready = sem("pooled_ready")
        grp_filled = sem("grp_filled")
        grp_taken = sem("grp_taken")
        out_filled = sem("out_filled")
        logits_filled = sem("logits_filled")
        scores_ready = sem("scores_ready")
        sel_ready = sem("sel_ready")
        pos_filled = sem("pos_filled")
        need_ready = sem("need_ready")
        rank_filled = sem("rank_filled")
        pick_ready = sem("pick_ready")
        list_filled = sem("list_filled")
        ctl_ready = sem("ctl_ready")
        shared_filled = sem("shared_filled")
        shared_silu = sem("shared_silu")
        shared_hidden = sem("shared_hidden")
        stored = sem("stored")

        class Flow:

            def __init__(self, tag):
                self.base = 0
                self.hot_ready = sem(f"{tag}_hot_ready")
                self.gather_filled = sem(f"{tag}_gather_filled")
                self.gather_taken = sem(f"{tag}_gather_taken")
                self.turn_filled = sem(f"{tag}_turn_filled")
                self.turn_taken = sem(f"{tag}_turn_taken")
                self.up_filled = sem(f"{tag}_up_filled")
                self.silu_ready = sem(f"{tag}_silu_ready")
                self.hidden_ready = sem(f"{tag}_hidden_ready")
                self.hidT_filled = sem(f"{tag}_hidT_filled")
                self.hidT_taken = sem(f"{tag}_hidT_taken")
                self.down_filled = sem(f"{tag}_down_filled")
                self.y_high = sem(f"{tag}_y_high")
                self.y_split = sem(f"{tag}_y_split")
                self.slotw_ready = sem(f"{tag}_slotw_ready")
                self.scattered = sem(f"{tag}_scattered")

        main = [Flow(f"main{l}") for l in range(2)]
        more = [Flow(f"more{l}") for l in range(2)]
        more_up_free = [sem(f"more{l}_up_free") for l in range(2)]
        more_down_free = [sem(f"more{l}_down_free") for l in range(2)]
        more_landed = [[sem(f"more{l}_landed{s}") for s in range(3)] for l in range(2)]

        PIECES = ([("gate", m) for m in range(4)] + [("val", m) for m in range(4)]
                  + [("v", i) for i in range(4)] + [("k", m) for m in range(4)] + [("q", m) for m in range(4)])
        NACT_EVEN = 16

        ADA_FOLDS = [0, 2, 4, 6] + list(range(8, 16))
        ADA_ROWS = [1, 3, 5, 7] + list(range(16, 24))
        even_in = [("in", 0, i) for i in (8, 9, 6, 7, 4, 5, 2, 3, 0, 1)]
        even_units = ([("ada", 0, i) for i in range(8)]
                      + [unit for i in range(8) for unit in (even_in[i], ("ada", 0, 8 + i))] + even_in[8:]
                      + [("ada", 0, i) for i in range(16, 24)] + [("out", 0, i) for i in range(4)]
                      + [("shared", 0, i) for i in range(3)])
        odd_units = ([("in", 1, i) for i in range(4)] + [("grp", 1, 0)] + [("out", 1, i) for i in range(4)]
                     + [("shared", 1, i) for i in range(3)])
        first_slot = [(-len(even_units)) % NSLOT, 6]
        occupant = [None] * NSLOT
        uses = [0] * NSLOT
        schedule = []
        at = {}

        def last_use(unit, position):
            kind, l, i = unit
            if kind == "ada":
                return (ada_used, ADA_FOLDS.index(i) + 1) if i in ADA_FOLDS else (ada_row_filled, ADA_ROWS.index(i) + 1)
            if kind == "in":
                return proj_filled, len(PIECES) * l + 2 * (position + 1)
            if kind == "grp":
                return grp_filled, KD
            if kind == "out":
                return (out_used, 3 * l + i + 1) if i < 3 else (out_filled, 4 * (l + 1))
            return (shared_filled, l + 1) if i == 1 else (shared_used, 2 * l + 1 + i // 2)

        expert_uses = []
        for l, units in enumerate((even_units, odd_units)):
            rows, ins_seen = [], 0
            for n, unit in enumerate(units):
                s = (first_slot[l] + n) % NSLOT
                uses[s] += 1
                rows.append((unit, s, 16 * uses[s], occupant[s]))
                at[unit] = (s, 16 * uses[s])
                occupant[s] = last_use(unit, ins_seen)
                ins_seen += unit[0] == "in"
            schedule.append(rows)
            expert_uses.append(list(uses))
            before_experts = list(occupant)
            rows.append(before_experts)
            for s in range(NSLOT):
                uses[s] += PAIRS // 2
                occupant[s] = "more" if s < 3 else (main[l].down_filled, PAIRS - 1 if s < 6 else PAIRS)

        def unit_source(unit):
            kind, l, i = unit
            if kind == "ada":
                return ada_w[l].rearrange("(p k) n -> p k n", k=KD)[:, :, i * UC:(i + 1) * UC]
            if kind == "in":
                w = ev_w_in if l == 0 else od_w_in
                return w.rearrange("(p k) n -> p k n", k=KD)[:, :, i * UC:(i + 1) * UC]
            if kind == "out":
                w = ev_w_out if l == 0 else od_w_out
                return w.rearrange("(i r p) n -> i p r n", r=2, p=P)[i]
            if kind == "grp":
                return od_w_grp.rearrange("g (r p) n -> p (g r) n", p=P)
            return (s1, s3, s2)[i][l].rearrange("(p k) n -> p (k n)", p=P)

        def slot_view(s, rows):
            return ring[:, s, :].rearrange("p (k n) -> p k n", k=rows)

        def piece_bank(i):
            return PS[:, (0, 1, 5, 6)[i % 4], 0:T]

        block = ctx.enter_context(nc.Block())

        @block.sync
        def _(sp):
            sp.dma_start(x[:], x_d.rearrange("(c p) d -> p c d", p=P)).then_inc(x_landed, 16)

            last_trips = []

            def wait_occupant(who):
                if who == "more":
                    sp.wait_ge(more[0].down_filled, last_trips[0])
                elif who is not None:
                    sp.wait_ge(*who)

            PAIR_ORDER = ((0, 0), (0, 1), (1, 0), (1, 1), (0, 2), (1, 2))

            def load_pair(l, par, it=None, prev=None):
                f = main[l]
                for hf, i in PAIR_ORDER:
                    s = 6 * par + 3 * hf + i
                    if it is None:
                        wait_occupant(prev[s])
                        e = 2 * par + hf
                    else:
                        e = it * 4 + (2 * par + hf)
                        sp.wait_ge(f.up_filled if i < 2 else f.down_filled, it * 2 + (par - 1))
                    sp.dma_start(ring[:, s, :],
                                 (w1, w3, w2)[i][l, bass.ds(e, 1)].rearrange("o (p k) n -> p (o k n)", p=P)
                                 ).then_inc(landed[s], 16)

            def load_ada_next(pair, par, first):
                if not first:
                    sp.wait_ge(adab_used, pair - 1)
                sp.dma_start(adab[par].rearrange("p (k n) -> p k n", k=KD),
                             ada_w[1].rearrange("(p k) n -> p k n", k=KD)[:, :, bass.ds(pair * ADAC, ADAC)]
                             ).then_inc(adab_landed[par], 16)

            for l in range(2):
                rows = schedule[l]
                for unit, s, _, who in rows[:-1]:
                    wait_occupant(who)
                    dst = ring[:, s, :] if unit[0] == "shared" else slot_view(s, 2 if unit[0] == "out" else KD)
                    sp.dma_start(dst, unit_source(unit)).then_inc(landed[s], 16)
                prev = rows[-1]
                for par in range(2):
                    load_pair(l, par, prev=prev)
                if l == 0:
                    sp.wait_ge(split_ready, 1)
                    sp.wait_ge(shared_filled, 1)
                    for j in range(2):
                        load_ada_next(j, j, True)
                with sp.Fori(1, PAIRS // 2) as it:
                    for par in range(2):
                        load_pair(l, par, it)
                        if l == 0:
                            load_ada_next(it * 2 + par, par, False)
                f = main[l]
                sp.wait_ge(ctl_ready, l + 1)
                trips = sp.value_load(ctl[0:1, 0:1], min_val=1, max_val=LIST)
                last_trips.append(trips)
                with sp.Fori(0, trips) as i:
                    e = sp.value_load(ctl[0:1, bass.ds(i + (1 + LIST), 1)], min_val=0, max_val=E - 1)
                    for n, w in enumerate((w1, w3, w2)):
                        if n != 1:
                            sp.wait_ge((more_up_free if n == 0 else more_down_free)[l], i + 1)
                        sp.dma_start(ring[:, n, :], w[l, bass.ds(e, 1)].rearrange("o (p k) n -> p (o k n)", p=P)
                                     ).then_inc(more_landed[l][n], 16)
            sp.wait_ge(stored, 16 * TC)

        @block.gpsimd
        def _(pool):
            made = [0]

            def const(ins):
                ins.then_inc(pool_const, 1)
                made[0] += 1
                pool.wait_ge(pool_const, made[0])

            def put(dst, cmp, base, pattern, mult, fill=0.0):
                const(nc.gpsimd.affine_select(out=dst, in_=dst, compare_op=cmp, fill=fill, base=base,
                                              pattern=pattern, channel_multiplier=mult))

            nc.gpsimd.memset(acc[:], 0.0).then_inc(acc_zeroed, 1)
            nc.gpsimd.memset(eps[:], EPS).then_inc(eps_ready, 1)
            const(nc.gpsimd.memset(ident[:], 0.0))
            put(ident[:], ALU.not_equal, 0, [[-1, P]], 1, 1.0)
            const(nc.gpsimd.memset(suffix[:], 1.0))
            put(suffix[:], ALU.is_ge, 0, [[-1, P]], 1)
            const(nc.gpsimd.memset(before[:], 1.0))
            put(before[:], ALU.is_gt, 0, [[1, P]], -1)
            const(nc.gpsimd.memset(ones[:], 1.0))
            const(nc.gpsimd.memset(mean_w[:], 1.0 / CW))
            const(nc.gpsimd.memset(mask[:], 1.0))
            put(mask[:, 0:P], ALU.is_gt, 0, [[1, P]], -1)
            put(mask[:, 2 * P:3 * P], ALU.is_gt, 0, [[1, P]], -1)
            const(nc.gpsimd.memset(negmask[:], -1.0))
            put(negmask[:, 0:P], ALU.is_gt, 0, [[1, P]], -1)
            put(negmask[:, 2 * P:3 * P], ALU.is_gt, 0, [[1, P]], -1)
            const(nc.gpsimd.memset(u[:, :, 0:PADC], 0.0))
            const(nc.gpsimd.iota(slotno[:], pattern=[[1, E]], base=0, channel_multiplier=0,
                                allow_small_or_imprecise_dtypes=True))
            const(nc.gpsimd.iota(idcol[:, 0, :], pattern=[[0, 4]], base=0, channel_multiplier=1,
                                allow_small_or_imprecise_dtypes=True))
            const(nc.gpsimd.iota(idcol[:, 1, :], pattern=[[E, 4]], base=1 + E, channel_multiplier=1,
                                allow_small_or_imprecise_dtypes=True))
            const(nc.gpsimd.iota(blkno[:], pattern=[[BLK, 4]], base=BLK, channel_multiplier=0,
                                allow_small_or_imprecise_dtypes=True))
            const(nc.gpsimd.memset(lower[:], 1.0))
            nc.gpsimd.affine_select(out=lower[:], in_=lower[:], compare_op=ALU.is_gt, fill=0.0, base=0,
                                    pattern=[[1, GROUPS], [-1, GROUPS]], channel_multiplier=0).then_inc(consts, 1)
            pool.wait_ge(params_ready, 2)
            pool.wait_ge(gate_ready, 2)
            nc.gpsimd.memset(acc[:], 0.0).then_inc(acc_zeroed, 1)
            pool.wait_ge(acc_zeroed, 2)
            pool.dma_start(acc[0:1, :], ada_b[1:2, :]).then_inc(bias_landed[1], 16)
            pool.wait_ge(logits_filled, 1)
            pool.dma_start(wr[:].rearrange("p k e -> p (k e)"),
                           w_router[1].rearrange("(p k) e -> p (k e)", k=KD)).then_inc(router_landed, 16)
            pool.wait_ge(params_ready, 3)
            nc.gpsimd.memset(up[:, :, 0:PADP], 0.0)
            nc.gpsimd.iota(icnt[:], pattern=[[1, PADP]], base=1, channel_multiplier=0,
                                allow_small_or_imprecise_dtypes=True).then_inc(pool_consts, 1)
            pool.wait_ge(gate_ready, 4)
            pool.dma_start(acc[:, 0:D], final_g[0].partition_broadcast(P)).then_inc(final_landed, 16)

        @block.scalar
        def _(act):
            SMALL = 4
            act.dma_start(vec[:], vec_d).then_inc(small_landed, 16)
            act.dma_start(wr[:].rearrange("p k e -> p (k e)"),
                          w_router[0].rearrange("(p k) e -> p (k e)", k=KD)).then_inc(small_landed, 16)
            for l in range(2):
                act.dma_start(biasr[:, l, :], moe_bias[l].partition_broadcast(P)).then_inc(small_landed, 16)
            act.wait_ge(acc_zeroed, 1)
            act.dma_start(acc[0:1, :], ada_b[0:1, :]).then_inc(bias_landed[0], 16)
            own = Chain(act, act_step)

            def square_sums(n):
                if n == 0:
                    act.wait_ge(x_landed, 16)
                for c in range(TC):
                    ins = nc.scalar.activation(xn[:, c, :], x[:, c, :], ACT.Square, scale=float(D) ** -0.5,
                                               accum_out=stat[:, c:c + 1])
                    own.step(ins)
                own.wait()
                nc.scalar.activation(stat[:, 2:4], stat[:, 0:2], ACT.Sqrt, bias=eps[:, 0:1]).then_inc(rms_ready, 1)

            def modulate(n):
                if n == 0:
                    act.wait_ge(params_ready, 1)
                else:
                    act.wait_ge(params_ready, n + 1)
                for k in range(KD):
                    act.wait_ge(xT_filled, KD * n + 2 * (k // 2) + 2)
                    nc.scalar.activation(hT[:, k, :], PS[:, k // 2, (k % 2) * HB:(k % 2) * HB + HB], ACT.Identity,
                                         scale=scl[:, n % 2, k:k + 1], bias=shf[:, n % 2, k:k + 1]
                                         ).then_inc(hT_ready, 1)

            def copy_gates(l):
                for g in range(2):
                    act.wait_ge(gate_filled, 2 * l + g + 1)
                    nc.scalar.copy(gates[:, g, :].rearrange("p (b n) -> p b n", b=2), PS[:, 5:7, :]
                                   ).then_inc(gate_ready, 1)

            act.wait_ge(small_landed, 16 * SMALL)
            nc.scalar.activation(cond[:], vec[:, V_C:V_C + KD], ACT.Silu).then_inc(cond_ready, 1)
            act.wait_ge(eps_ready, 1)
            square_sums(0)
            modulate(0)

            for i, (kind, m) in enumerate(PIECES):
                if kind == "val":
                    continue
                act.wait_ge(proj_filled, i + 1)
                if kind == "gate":
                    ins = nc.scalar.activation(sig[:, m, :], piece_bank(i), ACT.Sigmoid)
                elif kind == "v":
                    ins = nc.scalar.copy(v[:, m % 2, (m // 2) * UC:(m // 2) * UC + UC], piece_bank(i))
                elif kind == "k":
                    ins = nc.scalar.copy(kT[:, m, :], piece_bank(i))
                else:
                    ins = nc.scalar.mul(qT[:, m, :], piece_bank(i), DH ** -0.5)
                ins.then_inc(proj_taken, 1)
            for b in range(2):
                if b:
                    act.wait_ge(att_filled, 2)
                for hh in range(4):
                    h = 4 * b + hh
                    act.wait_ge(z_filled, h + 1)
                    own.step(nc.scalar.activation(lg[:, hh, :], PS[:, 5 + h % 2, 0:384], ACT.Abs))
                    nc.scalar.copy(zs[:, hh, :], PS[:, 5 + h % 2, 0:384]).then_inc(z_taken, 1)
                own.wait()
                own.step(nc.scalar.activation(lg[:], lg[:], ACT.Exp, scale=-1.0))
                own.wait()
                nc.scalar.activation(lg[:], lg[:], ACT.Ln, bias=1.0).then_inc(softplus_ready, 1)
                act.wait_ge(suffix_taken, 4 * b + 4)
                nc.scalar.activation(zs[:], zs[:], ACT.Exp).then_inc(exp_ready, 1)
                for j in range(2 * b, 2 * b + 2):
                    act.wait_ge(att_filled, j + 1)
                    nc.scalar.copy(mixT[:, j, :], PS[:, 7, 0:T]).then_inc(att_taken, 1)
            act.wait_ge(conv_done, MC)
            nc.scalar.copy(cv[:].rearrange("p (b m) t -> p b (m t)", b=2), PS[:, 2:4, :]).then_inc(conv_copied, 1)
            act.wait_ge(centred, 1)
            nc.scalar.activation(cv[:], sig[:], ACT.Square).then_inc(squared, 1)
            act.wait_ge(ln_filled, 2)
            nc.scalar.activation(PS[:, 6, HB:2 * HB], PS[:, 6, 0:T], ACT.Sqrt, bias=eps[:, 0:1]).then_inc(ln_root, 1)
            act.wait_ge(ln_ready, 1)
            for m in range(MC):
                nc.scalar.activation(mixT[:, 4 + m, :], sig[:, m, :], ACT.Silu, scale=vec[:, V_LG + m:V_LG + m + 1],
                                     bias=vec[:, V_LB + m:V_LB + m + 1]).then_inc(conv_mix, 1)

            def gather_out(f, pr, par, j):
                act.wait_ge(f.gather_filled, (pr + f.base) * 2 + (j + 1))
                for k in range(4 * j, 4 * j + 4):
                    ins = nc.scalar.activation(xg[:, par, k, :], PS[:, 7, (k % 4) * P:(k % 4 + 1) * P],
                                               ACT.Identity, scale=scl[:, 1, k:k + 1], bias=shf[:, 1, k:k + 1])
                ins.then_inc(f.gather_taken, 1)

            def silu(f, pr, rows=P):
                act.wait_ge(f.up_filled, pr + (f.base + 1))
                nc.scalar.activation(hid[0:rows, :], PS[0:rows, 6, 0:FF], ACT.Silu).then_inc(f.silu_ready, 1)

            def turn_out(f, pr):
                act.wait_ge(f.turn_filled, pr + (f.base + 1))
                nc.scalar.copy(hotT[:], PS[:, 7, :].rearrange("p (c n) -> p c n", c=TC)[:, :, 0:TW]
                               ).then_inc(f.turn_taken, 1)

            def y_high(f, pr, rows=P):
                act.wait_ge(f.down_filled, pr + (f.base + 1))
                act.wait_ge(f.slotw_ready, pr + (f.base + 1))
                nc.scalar.activation(yh[0:rows, :].rearrange("p (b n) -> p b n", b=2), PS[0:rows, 4:6, :], ACT.Copy,
                                     scale=wslot[0:rows, 0:1]).then_inc(f.y_high, 1)

            def moe(l):
                square_sums(2 * l + 1)
                modulate(2 * l + 1)
                act.wait_ge(logits_filled, l + 1)
                nc.scalar.activation(sc[:], PS[:, 6, 0:TC * E].rearrange("p (c e) -> p c e", c=TC), ACT.Sigmoid
                                     ).then_inc(scores_ready, 1)
                act.wait_ge(shared_filled, l + 1)
                nc.scalar.activation(shs, PS[:, 4, :], ACT.Silu).then_inc(shared_silu, 1)
                f = main[l]
                for j in range(2):
                    gather_out(f, 0, 0, j)

                def pair(pr, par, last=False):
                    silu(f, pr)
                    if not last:
                        for j in range(2):
                            gather_out(f, pr + 1, 1 - par, j)
                    turn_out(f, pr)
                    y_high(f, pr)

                with act.Fori(0, PAIRS // 2 - 1) as it:
                    for par in range(2):
                        pair(it * 2 + par, par)
                pair(PAIRS - 2, 0)
                pair(PAIRS - 1, 1, last=True)
                g = more[l]
                act.wait_ge(ctl_ready, l + 1)
                trips = act.value_load(ctl[0:1, 0:1], min_val=1, max_val=LIST)
                with act.Fori(0, trips) as i:
                    act.wait_ge(g.gather_filled, i + 1)
                    for k in range(KD):
                        ins = nc.scalar.activation(xg[:, 0, k, 0:BLK], PS[:, 7, k * BLK:(k + 1) * BLK], ACT.Identity,
                                                   scale=scl[:, 1, k:k + 1], bias=shf[:, 1, k:k + 1])
                    ins.then_inc(g.gather_taken, 1)
                    silu(g, i, BLK)
                    turn_out(g, i)
                    y_high(g, i, BLK)

            copy_gates(0)
            act.wait_ge(xn_ready, 2)
            moe(0)

            act.wait_ge(xn_ready, 4)
            square_sums(2)
            modulate(2)
            for i in range(KD):
                act.wait_ge(proj_filled, len(PIECES) + i + 1)
                if i == 0:
                    act.wait_ge(pool_consts, 1)
                nc.scalar.copy(up[:, i, PADP:], piece_bank(i)).then_inc(proj_taken, 1)
            for i in range(KD):
                act.wait_ge(grp_filled, i + 1)
                nc.scalar.activation(mixT[:, i, :], piece_bank(i), ACT.Copy, scale=vec[:, V_OS + i:V_OS + i + 1]
                                     ).then_inc(grp_taken, 1)
            copy_gates(1)
            act.wait_ge(xn_ready, 6)
            moe(1)
            act.wait_ge(xn_ready, 8)
            square_sums(4)
            for c in range(TC):
                act.wait_ge(xn_ready, 9 + c)
                act.dma_start(out_d[c * P:(c + 1) * P, :], x[:, c, :]).then_inc(stored, 16)

        @block.vector
        def _(dve):
            own = Chain(dve, dve_step)
            V = nc.vector

            def scale_x(n):
                dve.wait_ge(rms_ready, n + 1)
                own.step(V.reciprocal(stat[:, 0:2], stat[:, 2:4]))
                own.wait()
                if n < 4:
                    for c in range(TC):
                        ins = V.tensor_scalar(xn[:, c, :], x[:, c, :], stat[:, c:c + 1], None, ALU.mult)
                    ins.then_inc(xn_ready, 1)

            def split_x(l):
                for c in range(TC):
                    src = x[:, c, :].rearrange("p (q k) -> p k q", k=KD)
                    own.step(V.tensor_scalar(xh[:, c, :, :], src, stat[:, c:c + 1], None, ALU.mult))
                    own.wait()
                    ins = V.scalar_tensor_tensor(out=xl[:, c, :, :], in0=src, scalar=stat[:, c:c + 1],
                                                 in1=xh[:, c, :, :].bitcast(F32), op0=ALU.mult, op1=ALU.subtract)
                ins.then_inc(split_ready, 1)

            def fold_ada(i):
                s, n = at[("ada", 0, i)]
                dve.wait_ge(landed[s], n)
                wv = slot_view(s, KD)
                cols = acc[:, i * UC:(i + 1) * UC]
                done = ADA_FOLDS.index(i)
                part = PS[:, 4, (done % 2) * HB:(done % 2) * HB + UC]
                if done >= 2:
                    dve.wait_ge(ada_used, done - 1)
                for k in range(KD):
                    if k:
                        own.wait()
                    ins = V.scalar_tensor_tensor(
                        out=cols if k == KD - 1 else part, in0=wv[:, k, :], scalar=cond[:, k:k + 1],
                        in1=cols if k == 0 else part, op0=ALU.mult, op1=ALU.add)
                    if k < KD - 1:
                        own.step(ins)
                ins.then_inc(ada_used, 1)

            def add_ada_rows(n, units, bank):
                dve.wait_ge(ada_row_filled, n)
                cols = acc[0:1, units[0] * UC:(units[-1] + 1) * UC]
                V.tensor_tensor(cols, cols, PS[0:1, bank, 0:len(units) * UC], ALU.add
                                ).then_inc(ada_row_added, len(units))

            def params(l, which):
                dve.wait_ge(params_filled, 2 * l + which + 1)
                gain = V_G1 if which == 0 else V_G2
                V.tensor_copy(shf[:, which, :], PS[:, 7, 0:KD])
                V.scalar_tensor_tensor(out=scl[:, which, :], in0=PS[:, 7, KD:2 * KD], scalar=1.0,
                                       in1=vec[:, gain + l * KD:gain + (l + 1) * KD], op0=ALU.add, op1=ALU.mult
                                       ).then_inc(params_ready, 1)

            def residual(l, which):
                dve.wait_ge(gate_ready, 2 * l + which + 1)
                for c in range(TC):
                    for h in range(2):
                        b = 2 * c + h
                        if which == 0:
                            dve.wait_ge(out_filled, 4 * l + b + 1)
                        cols = slice(h * 512, (h + 1) * 512)
                        own.step(V.tensor_tensor(xn[:, c, cols], PS[:, b, :], gates[:, which, cols], ALU.mult))
                for c in range(TC):
                    for h in range(2):
                        cols = slice(h * 512, (h + 1) * 512)
                        own.wait(own.n if (c, h) == (1, 1) else own.n - 3 + 2 * c + h)
                        ins = V.tensor_tensor(x[:, c, cols], x[:, c, cols], xn[:, c, cols], ALU.add)
                ins.then_inc(xn_ready, 1)

            def route(l):
                dve.wait_ge(scores_ready, l + 1)
                own.step(V.tensor_tensor(bz[:], sc[:], biasr[:, l:l + 1, :].to_broadcast([P, TC, E]), ALU.add))
                own.wait()
                for c in range(TC):
                    for g in range(GROUPS):
                        ins = V.max(top[:, c * GROUPS + g, :], bz[:, c, g * PER:(g + 1) * PER])
                own.step(ins)
                own.wait()
                own.step(V.tensor_tensor(gsc[:], top[:, :, 0], top[:, :, 1], ALU.add))
                own.wait()
                for c in range(TC):
                    cs = slice(c * GROUPS, (c + 1) * GROUPS)
                    other = gsc[:, cs].unsqueeze(1).to_broadcast([P, GROUPS, GROUPS])
                    self_ = gsc[:, cs].unsqueeze(2).to_broadcast([P, GROUPS, GROUPS])
                    own.step(V.tensor_tensor(gcmp[:, cs, :], other, self_, ALU.is_gt))
                    own.step(V.tensor_tensor(geq[:, cs, :], other, self_, ALU.is_equal))
                    own.wait()
                    own.step(V.tensor_tensor(geq[:, cs, :], geq[:, cs, :], lower[:], ALU.mult))
                own.wait()
                own.step(V.tensor_tensor(gcmp[:], gcmp[:], geq[:], ALU.add))
                own.wait()
                own.step(V.tensor_reduce(grank[:], gcmp[:], AX_X, ALU.add))
                own.wait()
                own.step(V.tensor_scalar(grank[:], grank[:], TOPG - 0.5, None, ALU.is_lt))
                own.wait()
                own.step(V.tensor_scalar(goff[:], grank[:], BIG, -BIG, ALU.mult, ALU.add))
                own.wait()
                by_group = [P, TC * GROUPS, PER]
                bz_g = bz[:].rearrange("p c (g e) -> p (c g) e", e=PER)
                own.step(V.tensor_tensor(bz_g, bz_g, grank[:].unsqueeze(2).to_broadcast(by_group), ALU.mult))
                own.wait()
                own.step(V.tensor_tensor(bz_g, bz_g, goff[:].unsqueeze(2).to_broadcast(by_group), ALU.add))
                own.wait()
                for c in range(TC):
                    own.step(V.max(t8[:, c, :], bz[:, c, :]))
                own.wait()
                for c in range(TC):
                    own.step(V.match_replace(bz2[:, c, :], t8[:, c, :], bz[:, c, :], -3e38))
                own.wait()
                V.tensor_tensor(sel[:], bz[:], bz2[:], ALU.not_equal).then_inc(sel_ready, 1)
                split_x(l)
                if l == 0:
                    dve.wait_ge(consts, 1)
                for par in range(2):
                    for c in range(TC):
                        own.step(V.tensor_copy(idw[:, par, c, 0:P], ident[:]))
                dve.wait_ge(sel_ready, l + 1)
                own.step(V.tensor_tensor(wts[:], sel[:], sc[:], ALU.mult))
                own.wait()
                own.step(V.tensor_reduce(wsum[:], wts[:], AX_X, ALU.add))
                own.wait()
                own.step(V.reciprocal(wsum[:], wsum[:]))
                own.wait()
                for c in range(TC):
                    own.step(V.tensor_scalar(wts[:, c, :], wts[:, c, :], wsum[:, c:c + 1], ROUTED_SCALE,
                                             ALU.mult, ALU.mult))
                own.wait()
                own.step(V.tensor_copy(wsp[:, :, 0, :], wts[:]))
                own.wait()
                own.step(V.tensor_tensor(wsp[:, :, 1, :], wts[:], wsp[:, :, 0, :].bitcast(F32), ALU.subtract))
                dve.wait_ge(pos_filled, l + 1)
                w0 = where[:, :, 1:1 + E]
                own.step(V.scalar_tensor_tensor(out=w0, in0=PS[:, 6, HB:HB + TC * E].rearrange("p (c e) -> p c e", c=TC),
                                                scalar=1.0, in1=sel[:], op0=ALU.add, op1=ALU.mult))
                own.step(V.memset(where[:, :, 0:1], -1.0))
                own.wait()
                own.step(V.tensor_scalar(w0, w0, -1.0, None, ALU.add))
                own.wait()

            def block_list(l):
                own.step(V.tensor_copy(need[0:E, 6:7], PS[0:E, 6, HB + P:HB + P + 1]))
                for b in range(1, NBLK):
                    own.step(V.tensor_scalar(where[:, :, 1 + b * E:1 + (b + 1) * E], where[:, :, 1:1 + E],
                                             -float(BLK * b), None, ALU.add))
                own.wait()
                own.step(V.tensor_scalar(need[0:E, 0:3], blkno[0:E, 0:3], need[0:E, 6:7], None, ALU.is_lt))
                own.step(V.memset(need[0:E, 3:4], 0.0))
                own.wait()
                own.step(V.tensor_copy(need[0:E, 4:5], need[0:E, 0:1]))
                V.tensor_tensor(need[0:E, 5:6], need[0:E, 0:1], need[0:E, 1:2], ALU.add).then_inc(need_ready, 1)
                dve.wait_ge(rank_filled, l + 1)
                own.step(V.scalar_tensor_tensor(out=rank[0:E, 0:3], in0=PS[0:E, 4, 0:3], scalar=1.0,
                                                in1=need[0:E, 0:3], op0=ALU.add, op1=ALU.mult))
                own.wait()
                own.step(V.tensor_scalar(rank[0:E, 0:3], rank[0:E, 0:3], -1.0, None, ALU.add))
                own.wait()
                for b in range(3):
                    ins = V.tensor_scalar(pick[0:E, b, :], slotno[0:E, :], rank[0:E, b:b + 1], None, ALU.is_equal)
                ins.then_inc(pick_ready, 1)
                dve.wait_ge(list_filled, l + 1)
                own.step(V.tensor_reduce(ctlf[0:1, 0:1], PS[0:1, 4, 256:259], AX_X, ALU.add))
                own.wait()
                own.step(V.tensor_scalar(ctl[0:1, 0:1], ctlf[0:1, 0:1], 1.0, None, ALU.max))
                V.tensor_copy(ctl[0:1, 1:1 + 2 * LIST], PS[0:1, 4, 8:8 + 2 * LIST]).then_inc(ctl_ready, 1)

            def one_hot(f, pr, par, wait_turn):
                if wait_turn:
                    dve.wait_ge(f.turn_filled, pr + (f.base - 1))
                for c in range(TC):
                    for hf in range(2):
                        V.tensor_scalar(hot[:, par, c, hf * BLK:(hf + 1) * BLK], slotno[:],
                                        where[:, c, bass.ds(pr * 2 + (1 + hf), 1)], None, ALU.is_equal)
                for c in range(TC):
                    ins = V.tensor_copy(idw[:, par, c, P:TW].rearrange("p (s e) -> p s e", s=2),
                                        wsp[:, c, :, bass.ds(pr * 2, 2)].bitcast(F32))
                ins.then_inc(f.hot_ready, 1)

            def one_hot_more(f, i):
                code = dve.value_load(ctl[0:1, bass.ds(i + 1, 1)], min_val=0, max_val=NBLK * E)
                e = dve.value_load(ctl[0:1, bass.ds(i + (1 + LIST), 1)], min_val=0, max_val=E - 1)
                for c in range(TC):
                    V.tensor_scalar(hot[:, 0, c, 0:BLK], slotno[:], where[:, c, bass.ds(code, 1)], None, ALU.is_equal)
                for c in range(TC):
                    ins = V.tensor_copy(idw[:, 0, c, P:TW].rearrange("p (s e) -> p s e", s=2)[:, :, 0:1],
                                        wsp[:, c, :, bass.ds(e, 1)].bitcast(F32))
                ins.then_inc(f.hot_ready, 1)

            def hidden(f, pr, rows=P):
                dve.wait_ge(f.silu_ready, pr + (f.base + 1))
                V.tensor_tensor(hid[0:rows, :], PS[0:rows, 6, FF:2 * FF], hid[0:rows, :], ALU.mult
                                ).then_inc(f.hidden_ready, 1)
                dve.wait_ge(f.hidT_filled, pr + (f.base + 1))
                V.tensor_copy(hidT[:, :, 0:rows], PS[:, 6, 0:2 * P].rearrange("p (m s) -> p m s", m=2)[:, :, 0:rows]
                              ).then_inc(f.hidT_taken, 1)

            def slot_weights(f, pr, halves=2):
                dve.wait_ge(f.turn_taken, pr + (f.base + 1))
                for hf in range(halves):
                    rows = slice(hf * BLK, (hf + 1) * BLK)
                    parts = hotT[rows, :, P + hf:TW:2].bitcast(F32)
                    ins = V.tensor_reduce(wslot[rows, :], parts, mybir.AxisListType.XY, ALU.add)
                ins.then_inc(f.slotw_ready, 1)

            def y_low(f, pr, rows=P):
                dve.wait_ge(f.y_high, pr + (f.base + 1))
                V.scalar_tensor_tensor(out=yl[0:rows, :].rearrange("p (b n) -> p b n", b=2), in0=PS[0:rows, 4:6, :],
                                       scalar=wslot[0:rows, 0:1],
                                       in1=yh[0:rows, :].bitcast(F32).rearrange("p (b n) -> p b n", b=2),
                                       op0=ALU.mult, op1=ALU.subtract).then_inc(f.y_split, 1)

            def fold_ada_next(pr, par):
                dve.wait_ge(adab_landed[par], (pr - par) * 8 + 16)
                wv = adab[par].rearrange("p (k n) -> p k n", k=KD)
                cols = acc[:, bass.ds(pr * ADAC, ADAC)]
                for k in range(KD):
                    if k:
                        dve.wait_ge(ada_step, pr * (KD - 1) + k)
                    ins = V.scalar_tensor_tensor(out=cols if k == KD - 1 else adat[:], in0=wv[:, k, :],
                                                 scalar=cond[:, k:k + 1], in1=cols if k == 0 else adat[:],
                                                 op0=ALU.mult, op1=ALU.add)
                    ins.then_inc(ada_step if k < KD - 1 else adab_used, 1)

            def moe(l):
                f = main[l]
                scale_x(2 * l + 1)
                route(l)
                one_hot(f, 0, 0, False)
                one_hot(f, 1, 1, False)
                dve.wait_ge(shared_silu, l + 1)
                V.tensor_tensor(shid.rearrange("p m t -> p (m t)"), PS[:, 5, :], shs, ALU.mult
                                ).then_inc(shared_hidden, 1)
                block_list(l)

                def pair(pr, par, more_to_come=True):
                    hidden(f, pr)
                    if l == 0:
                        fold_ada_next(pr, par)
                    slot_weights(f, pr)
                    if more_to_come:
                        one_hot(f, pr + 2, par, True)
                    y_low(f, pr)

                if l == 0:
                    dve.wait_ge(bias_landed[1], 16)
                with dve.Fori(0, PAIRS // 2 - 1) as it:
                    for par in range(2):
                        pair(it * 2 + par, par)
                pair(PAIRS - 2, 0, False)
                pair(PAIRS - 1, 1, False)
                g = more[l]
                trips = dve.value_load(ctl[0:1, 0:1], min_val=1, max_val=LIST)
                dve.wait_ge(f.turn_filled, PAIRS + f.base)
                own.step(V.memset(hot[:, 0, :, BLK:P].bitcast(F32), 0.0))
                own.wait()
                with dve.Fori(0, trips) as i:
                    one_hot_more(g, i)
                    hidden(g, i, BLK)
                    slot_weights(g, i, 1)
                    y_low(g, i, BLK)
                dve.wait_ge(g.scattered, trips)
                residual(l, 1)

            dve.wait_ge(cond_ready, 1)
            dve.wait_ge(bias_landed[0], 16)
            fold_ada(0)
            scale_x(0)
            fold_ada(2)
            fold_ada(4)
            for n in range(2):
                add_ada_rows(n + 1, [ADA_ROWS[n]], 5 + n)
            fold_ada(6)
            for n in range(2, 4):
                add_ada_rows(n + 1, [ADA_ROWS[n]], (7, 5)[n - 2])
            params(0, 0)
            for i in range(8, 12):
                fold_ada(i)
            for m in range(MC):
                dve.wait_ge(proj_taken, m + 1)
                dve.wait_ge(proj_filled, 4 + m + 1)
                V.tensor_tensor(u[:, m, PADC:], piece_bank(4 + m), sig[:, m, :], ALU.mult).then_inc(conv_in, 1)
            dve.wait_ge(conv_in, MC)

            def conv_tap(j):
                for m in range(MC):
                    y = PS[:, 2 + m // 2, (m % 2) * HB:(m % 2) * HB + HB]
                    tap = vec[:, V_DW + m * TAPS + j:V_DW + m * TAPS + j + 1]
                    if j == 0:
                        own.step(V.tensor_scalar(y, u[:, m, 0:T], tap, vec[:, V_DB + m:V_DB + m + 1], ALU.mult, ALU.add))
                    else:
                        own.wait(taps_at[m])
                        ins = V.scalar_tensor_tensor(out=y, in0=u[:, m, j:j + T], scalar=tap, in1=y,
                                                     op0=ALU.mult, op1=ALU.add)
                        if j == TAPS - 1:
                            ins.then_inc(conv_done, 1)
                            continue
                        own.step(ins)
                    taps_at[m] = own.n

            taps_at = [0] * MC

            def log_gates(b):
                dve.wait_ge(softplus_ready, b + 1)
                own.step(V.scalar_tensor_tensor(out=lg[:], in0=zs[:], scalar=0.0, in1=lg[:], op0=ALU.max, op1=ALU.add))
                own.wait()
                V.tensor_tensor(lg[:], lg[:], negmask[:].unsqueeze(1).to_broadcast([P, 4, 384]), ALU.mult
                                ).then_inc(logm_ready, 1)

            def exponents(b):
                for hh in range(4):
                    h = 4 * b + hh
                    dve.wait_ge(suffix_filled, h + 1)
                    V.tensor_tensor(zs[:, hh, :], zs[:, hh, :], PS[:, h % 2, 0:384], ALU.add).then_inc(suffix_taken, 1)

            def probabilities(b):
                dve.wait_ge(exp_ready, b + 1)
                V.scalar_tensor_tensor(out=zs[:], in0=zs[:], scalar=1.0,
                                       in1=mask[:].unsqueeze(1).to_broadcast([P, 4, 384]),
                                       op0=ALU.min, op1=ALU.mult).then_inc(probs_ready, 1)

            between = {2: (fold_ada, 12), 5: (fold_ada, 13), 8: (fold_ada, 14), 11: (fold_ada, 15)}
            for j in range(TAPS):
                conv_tap(j)
                if j in between:
                    step, arg = between[j]
                    step(arg)
                if j == LOG0:
                    log_gates(0)
                if j == LOG0 + 1:
                    exponents(0)
                    add_ada_rows(6, ADA_ROWS[4:6], 4)
                if j == LOG0 + 4:
                    probabilities(0)
                    add_ada_rows(8, ADA_ROWS[6:8], 4)
            log_gates(1)
            exponents(1)
            add_ada_rows(10, ADA_ROWS[8:10], 4)
            probabilities(1)
            add_ada_rows(12, ADA_ROWS[10:12], 4)
            dve.wait_ge(ln_filled, 1)
            dve.wait_ge(conv_copied, 1)
            V.tensor_tensor(sig[:], cv[:], PS[:, 5, 0:T].unsqueeze(1).to_broadcast([P, MC, T]), ALU.subtract
                            ).then_inc(centred, 1)
            dve.wait_ge(ln_root, 1)
            own.step(V.reciprocal(PS[:, 4, HB:2 * HB], PS[:, 6, HB:2 * HB]))
            own.wait()
            dve.wait_ge(squared, 1)
            V.tensor_tensor(sig[:], sig[:], PS[:, 4, HB:2 * HB].unsqueeze(1).to_broadcast([P, MC, T]), ALU.mult
                            ).then_inc(ln_ready, 1)
            params(0, 1)
            residual(0, 0)
            moe(0)

            scale_x(2)
            params(1, 0)
            dve.wait_ge(pool_consts, 1)
            own.step(V.reciprocal(icnt[:], icnt[:]))
            for m in range(KD):
                g = m // 2
                dve.wait_ge(proj_taken, NACT_EVEN + m + 1)
                src, step = up[:, m, :], 1
                for n in range(g + 1):
                    lo = 1 if n == 0 else 2 ** (n + 1)
                    own.step(V.tensor_tensor(win[:, n, lo:], src[:, lo:], src[:, lo - step:PADP + T - step], ALU.add))
                    own.wait()
                    src, step = win[:, n, :], 2 * step
                w = WINDOWS[g]
                own.step(V.scalar_tensor_tensor(out=pooled[:, m, :], in0=src[:, PADP:], scalar=1.0 / w,
                                                in1=up[:, m, PADP:], op0=ALU.mult, op1=ALU.subtract))
                own.step(V.tensor_tensor(fix[:, 0:w], src[:, PADP:PADP + w], icnt[:, 0:w], ALU.mult))
                own.wait()
                V.tensor_tensor(pooled[:, m, 0:w], fix[:, 0:w], up[:, m, PADP:PADP + w], ALU.subtract
                                ).then_inc(pooled_ready, 1)
            params(1, 1)
            residual(1, 0)
            moe(1)
            dve.wait_ge(final_landed, 16)
            scale_x(4)
            for c in range(TC):
                own.step(V.tensor_scalar(xn[:, c, :], x[:, c, :], stat[:, c:c + 1], None, ALU.mult))
                own.wait()
                V.tensor_tensor(x[:, c, :], xn[:, c, :], acc[:, 0:D], ALU.mult).then_inc(xn_ready, 1)

        @block.tensor
        def _(pe):
            M = nc.tensor.matmul

            def transposes(n):
                pe.wait_ge(xn_ready, 2 * n + 1)
                if n == 0:
                    pe.wait_ge(consts, 1)
                for k in range(KD):
                    for c in range(TC):
                        o = (k % 2) * HB + c * P
                        ins = nc.tensor.transpose(PS[:, k // 2, o:o + P], xn[:, c, k::KD], ident[:])
                    ins.then_inc(xT_filled, 1)

            def param_columns(l, which):
                for s in range(2):
                    sec = 3 * which + s
                    for k in range(KD):
                        ins = M(PS[:, 7, s * KD + k:s * KD + k + 1], acc[:, sec * D + k:(sec + 1) * D:KD],
                                ones[:, 0:1], start=True, stop=True)
                ins.then_inc(params_filled, 1)

            def gate_rows(l):
                for g in range(2):
                    if g:
                        pe.wait_ge(gate_ready, 2 * l + 1)
                    for h in range(2):
                        o = (2 + 3 * g) * D + h * 512
                        ins = M(PS[:, 5 + h, :], ones[:], acc[:, o:o + 512], start=True, stop=True)
                    ins.then_inc(gate_filled, 1)

            def landed_wait(unit):
                s, n = at[unit]
                pe.wait_ge(landed[s], n)
                return s

            def project(n, l, units, pieces, taken):
                pe.wait_ge(hT_ready, KD * (n + 1))
                for i, (unit, kind, sub) in enumerate(pieces):
                    s = landed_wait(unit)
                    wv = slot_view(s, KD)
                    if i >= 4:
                        taken(i - 4)
                    for k in range(KD):
                        if kind == "v":
                            ins = M(piece_bank(i), hT[:, k, sub * P:(sub + 1) * P], wv[:, k, :],
                                    start=(k == 0), stop=(k == KD - 1))
                        else:
                            ins = M(piece_bank(i), wv[:, k, sub * P:(sub + 1) * P], hT[:, k, :],
                                    start=(k == 0), stop=(k == KD - 1))
                    ins.then_inc(proj_filled, 1)

            def output(l, ready):
                for i in range(4):
                    s = landed_wait(("out", l, i))
                    wv = slot_view(s, 2)
                    for r in range(2):
                        kk = 2 * i + r
                        ready(kk)
                        for c in range(TC):
                            for h in range(2):
                                ins = M(PS[:, 2 * c + h, :], mixT[:, kk, c * P:(c + 1) * P],
                                        wv[:, r, h * 512:(h + 1) * 512], start=(kk == 0), stop=(kk == KD - 1))
                                if kk == KD - 1:
                                    ins.then_inc(out_filled, 1)
                    if i < 3:
                        ins.then_inc(out_used, 1)

            def gather(f, par, j, bank_free):
                if bank_free:
                    pe.wait_ge(*bank_free)
                for k in range(4 * j, 4 * j + 4):
                    o, n = (k % 4) * P, 0
                    for c in range(TC):
                        for part in (xh, xl):
                            ins = M(PS[:, 7, o:o + P], part[:, c, k, :], hot[:, par, c, :],
                                    start=(n == 0), stop=(n == 3))
                            n += 1
                ins.then_inc(f.gather_filled, 1)

            def up(f, par, experts, freed=()):
                for slots in experts:
                    for _, sm, val in slots[0:2]:
                        pe.wait_ge(sm, val)
                for k in range(KD):
                    for hf, slots in enumerate(experts):
                        rows = slice(hf * BLK, (hf + 1) * BLK)
                        s = slots[0][0]
                        w13 = ring[:, s:s + 2, :].rearrange("p j (k n) -> p j k n", k=KD)
                        ins = M(PS[rows, 6, :], xg[:, par, k, rows], w13[:, :, k, :], start=(k == 0), stop=(k == KD - 1))
                        if k == 0 and hf < len(freed):
                            ins.then_inc(freed[hf], 1)
                ins.then_inc(f.up_filled, 1)

            def turn_hidden(f, hidden_at):
                pe.wait_ge(f.hidden_ready, hidden_at)
                for m in range(2):
                    ins = nc.tensor.transpose(PS[:, 6, m * P:(m + 1) * P], hid[:, m::2], ident[:])
                ins.then_inc(f.hidT_filled, 1)

            def turn(f, par, gather_at, freed=None):
                pe.wait_ge(f.gather_taken, gather_at)
                for c in range(TC):
                    ins = M(PS[:, 7, c * HB:c * HB + TW], hot[:, par, c, :], idw[:, par, c, :],
                            start=True, stop=True)
                    if freed is not None and c == 0:
                        ins.then_inc(freed, 1)
                ins.then_inc(f.turn_filled, 1)

            def down(f, experts, hidden_at):
                pe.wait_ge(f.hidT_taken, hidden_at)
                for slots in experts:
                    pe.wait_ge(slots[2][1], slots[2][2])
                for h in range(2):
                    for j in range(2):
                        for hf, slots in enumerate(experts):
                            rows = slice(hf * BLK, (hf + 1) * BLK)
                            ins = M(PS[rows, 4 + h, :], hidT[:, j, rows],
                                    slot_view(slots[2][0], 2)[:, j, h * 512:(h + 1) * 512],
                                    start=(j == 0), stop=(j == 1))
                ins.then_inc(f.down_filled, 1)

            def scatter(f, split_at, rows=P, freed=None):
                pe.wait_ge(f.y_split, split_at)
                for c in range(TC):
                    for h in range(2):
                        for part in (yh, yl):
                            ins = M(PS[:, 2 * c + h, :], hotT[0:rows, c, 0:P], part[0:rows, h * 512:(h + 1) * 512],
                                    start=False, stop=False, skip_group_check=True)
                            if freed is not None:
                                ins.then_inc(freed, 1)
                                freed = None
                ins.then_inc(f.scattered, 1)

            def moe(l):
                n = 2 * l + 1
                transposes(n)
                pe.wait_ge(hT_ready, KD * (n + 1))
                if l == 0:
                    pe.wait_ge(small_landed, 16 * 4)
                else:
                    pe.wait_ge(router_landed, 16)
                for c in range(TC):
                    for k in range(KD):
                        ins = M(PS[:, 6, c * E:(c + 1) * E], hT[:, k, c * P:(c + 1) * P], wr[:, k, :],
                                start=(k == 0), stop=(k == KD - 1))
                ins.then_inc(logits_filled, 1)
                for j in range(2):
                    s = landed_wait(("shared", l, j))
                    wv = slot_view(s, KD)
                    for m in range(2):
                        for k in range(KD):
                            ins = M(PS[:, 4 + j, m * HB:(m + 1) * HB], wv[:, k, m::2], hT[:, k, :],
                                    start=(k == 0), stop=(k == KD - 1))
                    if j == 0:
                        ins.then_inc(shared_used, 1)
                ins.then_inc(shared_filled, 1)
                pe.wait_ge(sel_ready, l + 1)
                pe.wait_ge(scores_ready, l + 1)
                for c in range(TC):
                    o = PS[:, 6, HB + c * E:HB + (c + 1) * E]
                    if c:
                        M(o, ones[:], sel[:, 0, :], start=True, stop=False)
                    M(o, before[:], sel[:, c, :], start=(c == 0), stop=True)
                for c in range(TC):
                    ins = M(PS[0:E, 6, HB + P:HB + P + 1], sel[:, c, :], ones[:, 0:1],
                            start=(c == 0), stop=(c == TC - 1))
                ins.then_inc(pos_filled, 1)
                f = main[l]
                B = f.base
                pe.wait_ge(f.hot_ready, B + 1)
                pe.wait_ge(split_ready, l + 1)
                for j in range(2):
                    gather(f, 0, j, (f.gather_taken, 2 * B + 1) if j else None)
                pe.wait_ge(shared_hidden, l + 1)
                s = landed_wait(("shared", l, 2))
                wv = slot_view(s, 2)
                for c in range(TC):
                    for h in range(2):
                        for j in range(2):
                            ins = M(PS[:, 2 * c + h, :], shid[:, j, c * P:(c + 1) * P],
                                    wv[:, j, h * 512:(h + 1) * 512], start=(j == 0), stop=(j == 1))
                ins.then_inc(shared_used, 1)
                pe.wait_ge(need_ready, l + 1)
                M(PS[0:E, 4, 0:3], before[0:E, 0:E], need[0:E, 0:3], start=True, stop=False)
                M(PS[0:E, 4, 0:3], ones[0:E, 0:E], need[0:E, 3:6], start=False, stop=True).then_inc(rank_filled, 1)
                pe.wait_ge(pick_ready, l + 1)
                for t in range(2):
                    for b in range(3):
                        M(PS[0:1, 4, 8 + t * LIST:8 + (t + 1) * LIST], idcol[0:E, 1 - t, b:b + 1], pick[0:E, b, :],
                          start=(b == 0), stop=(b == 2))
                M(PS[0:1, 4, 256:259], ones[0:E, 0:1], need[0:E, 0:3], start=True, stop=True).then_inc(list_filled, 1)

                def pair(pr, par, first=False, last=False):
                    def slot(hf, i):
                        s = 6 * par + 3 * hf + i
                        return s, landed[s], (pr - par) * 8 + (16 * expert_uses[l][s] + 16)
                    q = pr + B
                    experts = [[slot(hf, i) for i in range(3)] for hf in range(2)]
                    pe.wait_ge(f.gather_taken, q * 2 + 2)
                    up(f, par, experts, (more_up_free[l], more_down_free[l]) if last else ())
                    if not last:
                        pe.wait_ge(f.hot_ready, q + 2)
                        gather(f, 1 - par, 0, None if first else (f.turn_taken, q))
                    if not first:
                        scatter(f, q)
                    turn_hidden(f, q + 1)
                    if not last:
                        gather(f, 1 - par, 1, (f.gather_taken, q * 2 + 3))
                    if first:
                        pe.wait_ge(ctl_ready, l + 1)
                    down(f, experts, q + 1)
                    if last:
                        pe.wait_ge(f.turn_taken, q)
                    turn(f, par, q * 2 + (2 if last else 4))

                pair(0, 0, first=True)
                pair(1, 1)
                with pe.Fori(1, PAIRS // 2 - 1) as it:
                    for par in range(2):
                        pair(it * 2 + par, par)
                pair(PAIRS - 2, 0)
                pair(PAIRS - 1, 1, last=True)
                scatter(f, B + PAIRS)

                g = more[l]
                trips = pe.value_load(ctl[0:1, 0:1], min_val=1, max_val=LIST)
                pe.wait_ge(f.turn_taken, B + PAIRS)
                with pe.Fori(0, trips) as i:
                    def slot(n):
                        return n, more_landed[l][n], i * 16 + 16
                    pe.wait_ge(g.hot_ready, i + 1)
                    for k in range(KD):
                        n = 0
                        for c in range(TC):
                            for part in (xh, xl):
                                ins = M(PS[:, 7, k * BLK:(k + 1) * BLK], part[:, c, k, :], hot[:, 0, c, 0:BLK],
                                        start=(n == 0), stop=(n == 3))
                                n += 1
                    ins.then_inc(g.gather_filled, 1)
                    pe.wait_ge(g.gather_taken, i + 1)
                    experts = [[slot(n) for n in range(3)]]
                    up(g, 0, experts)
                    turn(g, 0, i + 1, more_up_free[l])
                    turn_hidden(g, i + 1)
                    down(g, experts, i + 1)
                    scatter(g, i + 1, BLK, more_down_free[l])

            def ada_rows(units, bank):
                for h, i in enumerate(units):
                    s = landed_wait(("ada", 0, i))
                    wv = slot_view(s, KD)
                    for k in range(KD):
                        ins = M(PS[0:1, bank, h * HB:h * HB + UC], cond[:, k:k + 1], wv[:, k, :],
                                start=(k == 0), stop=(k == KD - 1))
                    ins.then_inc(ada_row_filled, 1)

            pe.wait_ge(cond_ready, 1)
            ada_rows([1], 5)
            ada_rows([3], 6)
            transposes(0)
            ada_rows([5], 7)
            pe.wait_ge(ada_row_added, 1)
            ada_rows([7], 5)
            pe.wait_ge(ada_used, 4)
            pe.wait_ge(ada_row_added, 4)
            param_columns(0, 0)
            pieces = [(("in", 0, 8 + m // 2), "col", m % 2) for m in range(4)]
            pieces += [(("in", 0, 6 + m // 2), "col", m % 2) for m in range(4)]
            pieces += [(("in", 0, 4 + i // 2), "v", i % 2) for i in range(4)]
            pieces += [(("in", 0, 2 + m // 2), "col", m % 2) for m in range(4)]
            pieces += [(("in", 0, m // 2), "col", m % 2) for m in range(4)]

            def even_taken(i):
                if 4 <= i < 8:
                    pe.wait_ge(conv_in, i - 3)
                else:
                    pe.wait_ge(proj_taken, i + 1 if i < 4 else i - 3)

            project(0, 0, None, pieces, even_taken)
            pe.wait_ge(proj_taken, NACT_EVEN)
            for b in range(2):
                for h in range(4 * b, 4 * b + 4):
                    if h >= 2:
                        pe.wait_ge(z_taken, h - 1)
                    rows = slice(DH * (h % 2), DH * (h % 2) + DH)
                    M(PS[:, 5 + h % 2, 0:T], kT[rows, h // 2, 0:P], qT[rows, h // 2, :], start=True, stop=True)
                    M(PS[:, 5 + h % 2, T:T + P], kT[rows, h // 2, P:T], qT[rows, h // 2, P:T],
                      start=True, stop=True).then_inc(z_filled, 1)
                if b == 0:
                    pe.wait_ge(ada_used, len(ADA_FOLDS))
                else:
                    pe.wait_ge(ada_row_added, 8)
                ada_rows(ADA_ROWS[4 + 4 * b:6 + 4 * b], 4)
                pe.wait_ge(logm_ready, b + 1)
                for h in range(4 * b, 4 * b + 4):
                    hh = h % 4
                    if h >= 2:
                        pe.wait_ge(suffix_taken, h - 1)
                    o = PS[:, h % 2, :]
                    M(o[:, 0:T], suffix[:], lg[:, hh, 0:T], start=True, stop=False)
                    M(o[:, P:T], ones[:], lg[:, hh, T:T + P], start=False, stop=True)
                    M(o[:, T:T + P], suffix[:], lg[:, hh, T:T + P], start=True, stop=True).then_inc(suffix_filled, 1)
                pe.wait_ge(ada_row_added, 6 + 4 * b)
                ada_rows(ADA_ROWS[6 + 4 * b:8 + 4 * b], 4)
                pe.wait_ge(probs_ready, b + 1)
                for h in range(4 * b, 4 * b + 4):
                    hh, j = h % 4, h // 2
                    if j and h % 2 == 0:
                        pe.wait_ge(att_taken, j)
                    o = PS[DH * (h % 2):DH * (h % 2) + DH, 7, 0:T]
                    M(o, v[:, 0, h * DH:(h + 1) * DH], zs[:, hh, 0:T], start=True, stop=False)
                    ins = M(o[:, P:T], v[:, 1, h * DH:(h + 1) * DH], zs[:, hh, T:T + P], start=False, stop=True)
                    if h % 2:
                        ins.then_inc(att_filled, 1)
            pe.wait_ge(conv_copied, 1)
            for m in range(MC):
                ins = M(PS[:, 5, 0:T], mean_w[:], cv[:, m, :], start=(m == 0), stop=(m == MC - 1))
            ins.then_inc(ln_filled, 1)
            pe.wait_ge(squared, 1)
            for m in range(MC):
                ins = M(PS[:, 6, 0:T], mean_w[:], cv[:, m, :], start=(m == 0), stop=(m == MC - 1))
            ins.then_inc(ln_filled, 1)
            pe.wait_ge(ada_row_added, len(ADA_ROWS))
            pe.wait_ge(att_taken, 4)
            param_columns(0, 1)
            pe.wait_ge(ln_ready, 1)
            gate_rows(0)

            def even_ready(kk):
                if kk >= 4:
                    pe.wait_ge(conv_mix, kk - 3)

            output(0, even_ready)
            moe(0)

            pe.wait_ge(adab_used, PAIRS)
            param_columns(1, 0)
            transposes(2)

            def odd_taken(i):
                pe.wait_ge(proj_taken, NACT_EVEN + i + 1)

            project(2, 1, None, [(("in", 1, m // 2), "col", m % 2) for m in range(KD)], odd_taken)
            s = landed_wait(("grp", 1, 0))
            wv = slot_view(s, KD)
            for i in range(KD):
                g, n = i // 2, i % 2
                pe.wait_ge(pooled_ready, 2 * g + 2)
                pe.wait_ge(proj_taken, NACT_EVEN + KD)
                if i >= 4:
                    pe.wait_ge(grp_taken, i - 3)
                for r in range(2):
                    ins = M(piece_bank(i), wv[:, 2 * g + r, n * P:(n + 1) * P], pooled[:, 2 * g + r, :],
                            start=(r == 0), stop=(r == 1))
                ins.then_inc(grp_filled, 1)
            pe.wait_ge(params_ready, 3)
            param_columns(1, 1)
            pe.wait_ge(grp_taken, KD)
            gate_rows(1)
            output(1, lambda kk: None)
            moe(1)


_NAMES = ["x", "vec", "ada_w", "ada_b", "ev_w_in", "ev_w_out", "od_w_in", "od_w_grp", "od_w_out",
          "moe_w_router", "moe_bias", "moe_w1", "moe_w3", "moe_w2", "sh_w1", "sh_w3", "sh_w2", "final_g"]


def kernel(**inputs):
    import numpy as np
    import concourse.bacc as bacc
    from concourse.bass_utils import run_bass_kernel_spmd as run

    a = {n: np.ascontiguousarray(inputs[n]) for n in inputs}
    by_row = lambda w: w.reshape(P, KD)
    by_chunk = lambda w: w.reshape(-1, P).T
    cols = [by_row(a["c"][0])] + [by_row(a["norm1_g"][l]) for l in range(2)]
    cols += [by_row(a["norm2_g"][l]) for l in range(2)] + [by_chunk(a["od_scale"][0])]
    cols += [a["ev_dw_w"][0, :, 0, :].reshape(TAPS, MC, P).transpose(2, 1, 0).reshape(P, MC * TAPS)]
    cols += [by_chunk(a[n][0]) for n in ("ev_dw_b", "ev_ln_g", "ev_ln_b")]
    a["vec"] = np.ascontiguousarray(np.concatenate(cols, axis=1))
    a["x"] = a["x"][0]
    for n in ("ev_w_in", "ev_w_out", "od_w_in", "od_w_grp", "od_w_out"):
        a[n] = a[n][0]
    a["final_g"] = a["final_g"].reshape(1, D)

    nc = bacc.Bacc("TRN2", target_bir_lowering=False, num_devices=1)
    arrays, args = {}, []
    for name in _NAMES:
        arrays[f"in_{name}"] = np.ascontiguousarray(a[name])
        args.append(nc.dram_tensor(f"in_{name}", a[name].shape, mybir.dt.from_np(a[name].dtype),
                                   kind="ExternalInput").ap())
    args.append(nc.dram_tensor("out", (T, D), F32, kind="ExternalOutput").ap())
    trunk(nc, *args)
    r = run(nc, [arrays], core_ids=[0])
    return r.results[0]["out"].reshape(inputs["x"].shape)
```
